# Optimizing a Trainium2 kernel written in Bass

```python
import math
import jax, jax.numpy as jnp
from jax import lax
import numpy as np

D_MODEL = 1024
BATCH = 1
SEQ = 512
DEPTH = 2

CHUNK = 64
N_META = 16
SSM_GROUP = 16
SSM_GROUPS = D_MODEL // SSM_GROUP
SSM_STATE = 64
SSM_DT_MIN = 1e-3
SSM_DT_MAX = 1e-1
N_HEADS = 16
N_KV_HEADS = 4
HEAD_DIM = 64
Q_PER_KV = N_HEADS // N_KV_HEADS
WINDOW = 128
WINDOW_CHUNKS = WINDOW // CHUNK
QKV_DIM = (N_HEADS + 2 * N_KV_HEADS) * HEAD_DIM
D_FF = -(-8 * D_MODEL // (3 * 256)) * 256
RMS_EPS = 1e-5
NEG_INF = -1e30

kernel_name = "interleaved_s5_swa_sink_hybrid"

def rms_norm(x, g):
    xf = x.astype(jnp.float32)
    y = xf * lax.rsqrt(jnp.mean(xf * xf, axis=-1, keepdims=True) + RMS_EPS)
    return y.astype(x.dtype) * g

def swiglu_ffn(h, w_gate, w_up, w_down):
    return (jax.nn.silu(h @ w_gate) * (h @ w_up)) @ w_down

def _linear_recurrence_combine(left, right):
    a_l, b_l = left
    a_r, b_r = right
    return (a_l * a_r, a_r * b_l + b_r)

def s5_mixer(h, lam_re, lam_im, log_dt, b_re, b_im, c_re, c_im, d_skip, w_glu_a, w_glu_b):
    bsz, length, _ = h.shape
    u = h.astype(jnp.float32).reshape(bsz, length, SSM_GROUPS, SSM_GROUP)
    lam = lax.complex(jnp.minimum(lam_re.astype(jnp.float32), -1e-4),
                      lam_im.astype(jnp.float32))
    dt = jnp.exp(log_dt.astype(jnp.float32))[:, None]
    lam_bar = jnp.exp(lam * dt)
    b_mat = lax.complex(b_re.astype(jnp.float32), b_im.astype(jnp.float32))
    b_bar = ((lam_bar - 1.0) / lam)[..., None] * b_mat
    c_mat = lax.complex(c_re.astype(jnp.float32), c_im.astype(jnp.float32))
    bu = jnp.einsum('blgp,gnp->blgn', u, b_bar)
    a_seq = jnp.broadcast_to(lam_bar[None, None], (1, length, SSM_GROUPS, SSM_STATE))
    _, states = lax.associative_scan(_linear_recurrence_combine, (a_seq, bu), axis=1)
    y = jnp.real(jnp.einsum('blgn,gpn->blgp', states, c_mat))
    y = y + d_skip.astype(jnp.float32).reshape(SSM_GROUPS, SSM_GROUP) * u
    g = jax.nn.gelu(y.reshape(bsz, length, D_MODEL)).astype(h.dtype)
    return (g @ w_glu_a) * jax.nn.sigmoid(g @ w_glu_b)

def _shift_chunks(t, j):
    if j == 0:
        return t
    pad = [(0, 0)] * t.ndim
    pad[1] = (j, 0)
    return jnp.pad(t, pad)[:, :t.shape[1]]

def sink_window_attention(h, w_qkv, b_qkv, sinks, w_o, b_o):
    bsz, length, _ = h.shape
    seq = length - N_META
    n_chunks = seq // CHUNK
    qkv = h @ w_qkv + b_qkv
    q = qkv[..., :N_HEADS * HEAD_DIM].reshape(bsz, length, N_KV_HEADS, Q_PER_KV, HEAD_DIM)
    k = qkv[..., N_HEADS * HEAD_DIM:(N_HEADS + N_KV_HEADS) * HEAD_DIM].reshape(
        bsz, length, N_KV_HEADS, HEAD_DIM)
    v = qkv[..., (N_HEADS + N_KV_HEADS) * HEAD_DIM:].reshape(bsz, length, N_KV_HEADS, HEAD_DIM)
    scale = 1.0 / math.sqrt(HEAD_DIM)
    sink = sinks.astype(jnp.float32).reshape(N_KV_HEADS, Q_PER_KV)

    q_m, k_m, v_m = q[:, :N_META], k[:, :N_META], v[:, :N_META]
    s_mm = jnp.einsum('bqkgd,bmkd->bkgqm', q_m, k_m).astype(jnp.float32) * scale
    sink_mm = jnp.broadcast_to(sink[None, :, :, None, None], s_mm.shape[:-1] + (1,))
    p_mm = jax.nn.softmax(jnp.concatenate([s_mm, sink_mm], axis=-1), axis=-1)[..., :-1]
    out_m = jnp.einsum('bkgqm,bmkd->bqkgd', p_mm.astype(v.dtype), v_m)
    out_m = out_m.reshape(bsz, N_META, N_HEADS * HEAD_DIM)

    q_r = q[:, N_META:].reshape(bsz, n_chunks, CHUNK, N_KV_HEADS, Q_PER_KV, HEAD_DIM)
    k_r = k[:, N_META:].reshape(bsz, n_chunks, CHUNK, N_KV_HEADS, HEAD_DIM)
    v_r = v[:, N_META:].reshape(bsz, n_chunks, CHUNK, N_KV_HEADS, HEAD_DIM)
    shifts = list(range(WINDOW_CHUNKS - 1, -1, -1))
    k_band = jnp.concatenate([_shift_chunks(k_r, j) for j in shifts], axis=2)
    v_band = jnp.concatenate([_shift_chunks(v_r, j) for j in shifts], axis=2)
    band_shift = jnp.repeat(jnp.array(shifts, dtype=jnp.int32), CHUNK)
    band_valid = (jnp.arange(n_chunks, dtype=jnp.int32)[:, None] - band_shift[None, :]) >= 0

    s_meta = jnp.einsum('bcqkgd,bmkd->bckgqm', q_r, k_m).astype(jnp.float32) * scale
    s_band = jnp.einsum('bcqkgd,bcskd->bckgqs', q_r, k_band).astype(jnp.float32) * scale
    s_band = jnp.where(band_valid[None, :, None, None, None, :], s_band, NEG_INF)
    sink_r = jnp.broadcast_to(sink[None, None, :, :, None, None], s_meta.shape[:-1] + (1,))
    p = jax.nn.softmax(jnp.concatenate([s_meta, s_band, sink_r], axis=-1), axis=-1)
    p_meta = p[..., :N_META].astype(v.dtype)
    p_band = p[..., N_META:-1].astype(v.dtype)
    out_r = (jnp.einsum('bckgqm,bmkd->bcqkgd', p_meta, v_m)
             + jnp.einsum('bckgqs,bcskd->bcqkgd', p_band, v_band))
    out_r = out_r.reshape(bsz, seq, N_HEADS * HEAD_DIM)

    out = jnp.concatenate([out_m, out_r], axis=1)
    return out @ w_o + b_o

def setup_inputs(seed: int = 0) -> dict:
    key = jax.random.key(seed)
    ks = jax.random.split(key, 24)
    n_ssm = (DEPTH + 1) // 2
    n_att = DEPTH // 2
    f32 = jnp.float32
    nrm = lambda k, shape, s: jax.random.normal(k, shape, f32) * s
    n_idx = jnp.arange(SSM_STATE, dtype=f32)
    return {
        "x": nrm(ks[0], (BATCH, SEQ, D_MODEL), 1.0),
        "meta_tokens": nrm(ks[1], (N_META, D_MODEL), 1.0),
        "ln_mix": 1.0 + nrm(ks[2], (DEPTH, D_MODEL), 0.02),
        "ln_ffn": 1.0 + nrm(ks[3], (DEPTH, D_MODEL), 0.02),
        "ssm_lam_re": -0.5 + nrm(ks[4], (n_ssm, SSM_GROUPS, SSM_STATE), 0.01),
        "ssm_lam_im": math.pi * n_idx[None, None, :] + nrm(ks[5], (n_ssm, SSM_GROUPS, SSM_STATE), 0.01),
        "ssm_log_dt": jax.random.uniform(ks[6], (n_ssm, SSM_GROUPS), f32,
                                         minval=math.log(SSM_DT_MIN), maxval=math.log(SSM_DT_MAX)),
        "ssm_b_re": nrm(ks[7], (n_ssm, SSM_GROUPS, SSM_STATE, SSM_GROUP), (2 * SSM_GROUP) ** -0.5),
        "ssm_b_im": nrm(ks[8], (n_ssm, SSM_GROUPS, SSM_STATE, SSM_GROUP), (2 * SSM_GROUP) ** -0.5),
        "ssm_c_re": nrm(ks[9], (n_ssm, SSM_GROUPS, SSM_GROUP, SSM_STATE), SSM_STATE ** -0.5),
        "ssm_c_im": nrm(ks[10], (n_ssm, SSM_GROUPS, SSM_GROUP, SSM_STATE), SSM_STATE ** -0.5),
        "ssm_d": nrm(ks[11], (n_ssm, D_MODEL), 1.0),
        "ssm_w_glu_a": nrm(ks[12], (n_ssm, D_MODEL, D_MODEL), D_MODEL ** -0.5),
        "ssm_w_glu_b": nrm(ks[13], (n_ssm, D_MODEL, D_MODEL), D_MODEL ** -0.5),
        "attn_w_qkv": nrm(ks[14], (n_att, D_MODEL, QKV_DIM), D_MODEL ** -0.5),
        "attn_b_qkv": nrm(ks[15], (n_att, QKV_DIM), 0.02),
        "attn_sinks": nrm(ks[16], (n_att, N_HEADS), 0.5),
        "attn_w_o": nrm(ks[17], (n_att, N_HEADS * HEAD_DIM, D_MODEL), (N_HEADS * HEAD_DIM) ** -0.5),
        "attn_b_o": nrm(ks[18], (n_att, D_MODEL), 0.02),
        "ffn_w_gate": nrm(ks[19], (DEPTH, D_MODEL, D_FF), D_MODEL ** -0.5),
        "ffn_w_up": nrm(ks[20], (DEPTH, D_MODEL, D_FF), D_MODEL ** -0.5),
        "ffn_w_down": nrm(ks[21], (DEPTH, D_FF, D_MODEL), D_FF ** -0.5),
        "ln_f": 1.0 + nrm(ks[22], (D_MODEL,), 0.02),
    }

def reference(x, meta_tokens, ln_mix, ln_ffn, ssm_lam_re, ssm_lam_im, ssm_log_dt,
              ssm_b_re, ssm_b_im, ssm_c_re, ssm_c_im, ssm_d, ssm_w_glu_a, ssm_w_glu_b,
              attn_w_qkv, attn_b_qkv, attn_sinks, attn_w_o, attn_b_o,
              ffn_w_gate, ffn_w_up, ffn_w_down, ln_f):
    bsz = x.shape[0]
    meta = jnp.broadcast_to(meta_tokens.astype(x.dtype)[None], (bsz, N_META, D_MODEL))
    h_res = jnp.concatenate([meta, x], axis=1)
    for i in range(DEPTH):
        j = i // 2
        h = rms_norm(h_res, ln_mix[i])
        if i % 2 == 0:
            mix = s5_mixer(h, ssm_lam_re[j], ssm_lam_im[j], ssm_log_dt[j],
                           ssm_b_re[j], ssm_b_im[j], ssm_c_re[j], ssm_c_im[j],
                           ssm_d[j], ssm_w_glu_a[j], ssm_w_glu_b[j])
        else:
            mix = sink_window_attention(h, attn_w_qkv[j], attn_b_qkv[j], attn_sinks[j],
                                        attn_w_o[j], attn_b_o[j])
        h_res = h_res + mix
        h_res = h_res + swiglu_ffn(rms_norm(h_res, ln_ffn[i]),
                                   ffn_w_gate[i], ffn_w_up[i], ffn_w_down[i])
    out = rms_norm(h_res, ln_f)
    return out[:, N_META:]


_drawn_inputs = setup_inputs


def setup_inputs(seed=0):
    import zlib

    import numpy as np

    out = dict(_drawn_inputs(seed))
    spreads = {}
    factors = {'ln_mix': 5.061,
     'ln_ffn': 2.93,
     'ssm_lam_re': 64.0,
     'attn_b_qkv': 2.863,
     'attn_sinks': 64.0,
     'attn_b_o': 19.821,
     'ln_f': 7.964}
    for name, (base, spread) in spreads.items():
        noise = np.random.default_rng([zlib.crc32(name.encode()), seed]).standard_normal(out[name].shape)
        drawn = base * np.exp(spread * noise) if base else spread * noise
        out[name] = __import__('jax').numpy.asarray(drawn.astype(out[name].dtype))
    for name, factor in factors.items():
        out[name] = (out[name] * factor).astype(out[name].dtype)
    return out
```

```python
import math
from contextlib import ExitStack

import concourse.bass as bass
from concourse import mybir

F32 = mybir.dt.float32
F32R = mybir.dt.float32r
ALU = mybir.AluOpType
ACT = mybir.ActivationFunctionType
AX_X = mybir.AxisListType.X

P = 128
D = 1024
KB = D // P
SEQ, META = 512, 16
L = SEQ + META
HALF = L // 2
EPS = 1e-5

GROUPS, GROUP, STATE = 64, 16, 64
T = P // GROUP
C = L // T
CS = C - 1
PAIRS = GROUPS // 2
BATCHES = 8
TA = 8
PB = PAIRS // BATCHES
GB = 2 * PB
LOG2E = 1.0 / math.log(2.0)
ROUND = 1.5 * 2.0 ** 23
TWO_PI_HIGH = 6.28125
TWO_PI_LOW = 2 * math.pi - TWO_PI_HIGH
PI_BELOW = 3.1415925
ROW_NAMES = ("lam_bar_re", "lam_bar_im", "w_re", "w_im", "decay", "turn_re", "turn_im")

HEADS, KV_HEADS, HD = 16, 4, 64
HPK = HEADS // KV_HEADS
CHUNK = 64
QB = 2 * CHUNK
BLOCKS = SEQ // QB
BAND = 2 * CHUNK
WIN = META + BAND
WINDOWS = SEQ // CHUNK - 1
HALVES = ((0, 0), (0, 1), (1, 0), (1, 1))
STEPS = KV_HEADS * BLOCKS
WO_STEPS = (13, 15)
QUERY_STEPS = (0, 2, 4, 6, 8, 10)
SCALE = 1.0 / math.sqrt(HD)

FF = -(-8 * D // (3 * 256)) * 256
FB = FF // P
DOWN_TILES = ((0, 6), (6, 6), (12, 5), (17, 5))

QUAD_GLU, N_GLU = 0, 4
QUAD_UP = (4, 28)
N_UP = FB // 2
QUAD_DOWN = (QUAD_UP[0] + N_UP, QUAD_UP[1] + N_UP)
N_DOWN = 4
QUAD_KV = QUAD_DOWN[0] + 2 * N_DOWN
QUAD_Q = QUAD_KV + 1
QUAD_WO = QUAD_Q + 2
assert QUAD_WO + 2 == QUAD_UP[1]
LAST_BLOCK = 4 * (QUAD_DOWN[1] + 2 * N_DOWN) - 1

VEC = {"ln_ffn0": 0, "ln_mix1": 8, "ln_ffn1": 16, "ln_f": 24, "b_o": 32, "b_qkv": 40}
VECS = 52


def trunk(nc, x, meta_tokens, ln_mix, ln_ffn, lam_re, lam_im, log_dt, b_re, b_im, c_re, c_im,
          ssm_d, w_glu_a, w_glu_b, w_qkv, b_qkv, sinks, w_o, b_o, w_gate, w_up, w_down, ln_f, out):
    ctx = ExitStack()
    with ctx:
        def sb(name, shape, dt=F32, scope=ctx):
            return scope.enter_context(nc.sbuf_tensor(name, shape, dt))

        def sem(name):
            return ctx.enter_context(nc.semaphore(name))

        residual = sb("residual", [P, KB, L])
        raw = sb("raw", [P, 2, KB, 2 * P])
        w_high = sb("w_high", [P, 2, KB, P], F32R)
        skip = ExitStack()
        d_diag = sb("d_diag", [2 * GROUP, PAIRS, GROUP], scope=skip)
        skip.close()
        w_low = sb("w_low", [P, 2, KB, P], F32R)
        diag_mask = sb("diag_mask", [2 * GROUP, GROUP])
        ident = sb("ident", [P, P])
        ones = sb("ones", [P, P])
        neg_half = sb("neg_half", [P, 8])
        vecs_row = sb("vecs_row", [VECS, P])
        vecs = sb("vecs", [P, VECS])
        q_bias = sb("q_bias", [P, KB])
        sink_row = sb("sink_row", [P, HEADS])
        mean_sq = sb("mean_sq", [P, 8])
        rstd = sb("rstd", [P, 8])
        banks = ctx.enter_context(nc.psum_tensor("banks", [P, 8, 512], F32))
        y_dram = nc.dram_tensor("y_dram", (BATCHES, T, GROUP, GB, C), F32, kind="Internal").ap()

        early = ExitStack()
        row = {k: sb("row_" + k, [PAIRS, P], scope=early) for k in (
            "lam_re", "lam_im", "decay_arg", "angle", "turns", "abs_angle", "sin", "cos", "mag",
            "t0", "t1", "t2", "t3", "lr1") + ROW_NAMES}
        two = sb("two", [PAIRS, P], scope=early)
        dt_log = sb("dt_log", [PAIRS, 2], scope=early)
        dt_log2 = sb("dt_log2", [PAIRS, 2], scope=early)
        dt_row = sb("dt_row", [PAIRS, 2], scope=early)
        gain_row = sb("gain_row", [C, D], scope=early)
        early.close()
        gate = sb("gate", [P, 2, L])
        prod = sb("prod", [P, 2, L])
        square = sb("square", [P, L])
        sq_sum = sb("sq_sum", [P, L])
        rstd_row = sb("rstd_row", [P, L])
        diag = sb("diag", [P, L])

        tokens = ExitStack()
        xt = sb("xt", [C, T, D], scope=tokens)
        tokens.close()
        after_mixer = ExitStack()
        glu_high = sb("glu_high", [P, KB, L], F32R, scope=after_mixer)
        glu_low = sb("glu_low", [P, KB, L], F32R, scope=after_mixer)

        s5 = ExitStack()
        loaded = ExitStack()
        braw = {k: sb("raw_" + k, [PAIRS, 2 * STATE * GROUP], scope=loaded) for k in ("b_re", "b_im", "c_re", "c_im")}
        loaded.close()
        inj = sb("inj", [P, 2, PB, T, GROUP], scope=s5)
        inj_t = sb("inj_t", [P, PB, T, GROUP], scope=s5)
        inj_T = sb("inj_T", [P, PB, 2, P], scope=s5)
        read = sb("read", [P, 3, 2, PB, T + 1, GROUP], scope=s5)
        read_t = sb("read_t", [P, PB, T, GROUP], scope=s5)
        k_lag = sb("k_lag", [2 * GROUP, PB, T, GROUP], scope=s5)
        k_toep = sb("k_toep", [P, 2, GB, P], scope=s5)
        turn = sb("turn", [P, 2, 2, PB, CS], scope=s5)
        turn_t = sb("turn_t", [P, 2, PB, TA, TA], scope=s5)
        decay_row = sb("decay_row", [P, PB, CS], scope=s5)
        rows_only = ExitStack()
        u_row = sb("u_row", [C, 2, 16, T, GROUP], scope=rows_only)
        rows_only.close()
        z = sb("z", [P, 2, PB, CS], scope=s5)
        zt = sb("zt", [P, 2, PB, CS], scope=s5)
        zs = sb("zs", [P, 2, PB, CS], scope=s5)
        state = sb("state", [P, 2, PB, CS], scope=s5)
        y_act = sb("y_act", [P, 2, GB, C], scope=s5)
        y_feat = sb("y_feat", [P, 2, T, C], scope=s5)
        u_state = sb("u_state", [P, GROUPS, C], scope=s5)
        nat = {k: sb("nat_" + k, [P, PAIRS, GROUP], scope=s5) for k in ("b_re", "b_im", "c_re", "neg_c_im")}
        bbar_pair = sb("bbar_pair", [P, 2, PAIRS, 2 * GROUP], scope=s5)
        lam_t = sb("lam_t", [P, len(ROW_NAMES), PAIRS], scope=s5)
        powr = sb("powr", [P, 2, T + 1, PAIRS], scope=s5)
        fine = sb("fine", [P, 2, PAIRS, TA + 1], scope=s5)
        coarse = sb("coarse", [P, 2, PAIRS, TA + 1], scope=s5)
        pow_t = sb("pow_t", [P, 2, 4, PAIRS], scope=s5)
        s5.close()
        after_mixer.close()

        att = ExitStack()
        q_t = sb("q_t", [P, 2, 2, SEQ], scope=att)
        k_t = sb("k_t", [P, 2, 2, L], scope=att)
        v_t = sb("v_t", [P, 2, L], scope=att)
        v_meta_t = sb("v_meta_t", [P, 2, 4, 4 * META], scope=att)
        v_win = sb("v_win", [P, WINDOWS, KV_HEADS * HD], scope=att)
        v_meta = sb("v_meta", [4 * META, 4, KV_HEADS * HD], scope=att)
        prob_e = sb("prob_e", [P, 2, 2, WIN], scope=att)
        prob_b = sb("prob_b", [P, 2, 4, BAND], scope=att)
        prob_m = sb("prob_m", [P, 2, 4, META], scope=att)
        prob_tb = sb("prob_tb", [P, 2, 4, P], scope=att)
        prob_tm = sb("prob_tm", [4 * META, 2, P], scope=att)
        neg_sink = sb("neg_sink", [P, KV_HEADS, 2], scope=att)
        row_max = sb("row_max", [P, 2, 2], scope=att)
        neg_max = sb("neg_max", [P, 2, 2, 2], scope=att)
        sink_exp = sb("sink_exp", [P, 2, 2, 2], scope=att)
        denom = sb("denom", [P, 2, 2, 2], scope=att)
        o_high = sb("o_high", [P, KB, SEQ], F32R, scope=att)
        o_low = sb("o_low", [P, KB, SEQ], F32R, scope=att)
        att.close()

        fin = ExitStack()
        scaled = sb("scaled", [P, KB, SEQ], scope=fin)
        out_row = sb("out_row", [P, 4, D], scope=fin)
        fin.close()

        a_high = sb("a_high", [P, FB, L], F32R)
        a_low = sb("a_low", [P, FB, L], F32R)
        x_high = sb("x_high", [P, KB, L], F32R)
        x_low = sb("x_low", [P, KB, L], F32R)

        raw_loaded = [sem("raw_loaded0"), sem("raw_loaded1")]
        rows_loaded, bc_loaded, consts_loaded = sem("rows_loaded"), sem("bc_loaded"), sem("consts_loaded")
        x_loaded = [sem(f"x_loaded{i}") for i in range(4)]
        toep_placed, keys_swapped, out_stored = sem("toep_placed"), sem("keys_swapped"), sem("out_stored")
        w_rounded, w_split, w_used = sem("w_rounded"), sem("w_split"), sem("w_used")
        gate_ready, gate_scaled, pre_ready = sem("gate_ready"), sem("gate_scaled"), sem("pre_ready")
        up_taken, added, a_rounded, a_split = sem("up_taken"), sem("added"), sem("a_rounded"), sem("a_split")
        squared, sq_added = sem("squared"), sem("sq_added")
        mean_summed, mean_taken, rstd_ready = sem("mean_summed"), sem("mean_taken"), sem("rstd_ready")
        diag_ready, rstd_spread, rstd_copied = sem("diag_ready"), sem("rstd_spread"), sem("rstd_copied")
        x_rounded, x_split = sem("x_rounded"), sem("x_split")
        dve_step, pool_step, act_step = sem("dve_step"), sem("pool_step"), sem("act_step")
        consts_made, dt_ready, mag_ready, half_made = sem("consts_made"), sem("dt_ready"), sem("mag_ready"), sem("half_made")
        dt_arg, mag_arg, angle_ready, trig_ready, rows_ready = sem("dt_arg"), sem("mag_arg"), sem("angle_ready"), sem("trig_ready"), sem("rows_ready")
        vecs_t, vecs_ready, rows_t, rows_copied = sem("vecs_t"), sem("vecs_ready"), sem("rows_t"), sem("rows_copied")
        nat_tr, nat_copied, nat_ready = sem("nat_tr"), sem("nat_copied"), sem("nat_ready")
        x_squared, mean_ready0, rstd0 = sem("x_squared"), sem("mean_ready0"), sem("rstd0")
        res_t, res_copied, u_normed, u_tr, u_copied = sem("res_t"), sem("res_copied"), sem("u_normed"), sem("u_tr"), sem("u_copied")
        inj_ready, inj_tr, inj_copied = sem("inj_ready"), sem("inj_tr"), sem("inj_copied")
        turn_ready, read_ready, raw_c_copied = sem("turn_ready"), sem("read_ready"), sem("raw_c_copied")
        v_ready, v_taken, k_ready, k_copied, toep_cleared = sem("v_ready"), sem("v_taken"), sem("k_ready"), sem("k_copied"), sem("toep_cleared")
        turns_ready, k_ready_d, state_ready, y_ready, gelu_ready, y_placed, y_stored, bbar_placed = sem("turns_ready"), sem("k_ready_d"), sem("state_ready"), sem("y_ready"), sem("gelu_ready"), sem("y_placed"), sem("y_stored"), sem("bbar_placed")
        gt_rounded, gt_split, pairs_cleared = sem("gt_rounded"), sem("gt_split"), sem("pairs_cleared")
        kv_scaled, kv_ready, v_meta_ready, v_tr, v_rows_ready = sem("kv_scaled"), sem("kv_ready"), sem("v_meta_ready"), sem("v_tr"), sem("v_rows_ready")
        q_scaled, q_ready, scores_ready, shifted, prob_ready = sem("q_scaled"), sem("q_ready"), sem("scores_ready"), sem("shifted"), sem("prob_ready")
        prob_scaled, prob_tr, prob_t_ready = sem("prob_scaled"), sem("prob_tr"), sem("prob_t_ready")
        o_ready, o_rounded, o_split = sem("o_ready"), sem("o_rounded"), sem("o_split")
        scaled_ready, out_tr, out_copied = sem("scaled_ready"), sem("out_tr"), sem("out_copied")

        block = ctx.enter_context(nc.Block())

        def halves(n):
            return [(0, HALF), (HALF, HALF)] if n == L else [(META, SEQ)]

        def bank_view(first, n):
            return banks[:, first:first + 2, 0:HALF] if n == L else banks[:, first, 0:SEQ]

        def cols(ap, n):
            return ap.rearrange("p (h c) -> p h c", h=2) if n == L else ap[:, META:L]

        def norm_tiles(n):
            return (88, 6, 0) if n == L else (128, 4, META)

        def rows(ap, m, a=0, e=L):
            return ap[:, m, a:e] if isinstance(m, int) else ap[:, bass.ds(m, 1), a:e].rearrange("p o c -> p (o c)")

        def gain_of(name, m):
            return vecs[:, VEC[name] + m:VEC[name] + m + 1] if isinstance(m, int) else vecs[:, bass.ds(m + VEC[name], 1)]

        def rstd_banks(n):
            return banks[:, 6:8, 0:HALF] if n == L else banks[:, 7, :]

        def scores_of(s):
            b0 = 2 + 2 * (s % 2)
            return banks[:, b0:b0 + 2, 0:2 * WIN].rearrange("p h (c k) -> p h c k", c=2)

        def meta_of(s):
            return banks[0:4 * META, 2 + 2 * (s % 2), 2 * WIN:2 * WIN + P]

        def heads_out(o, s):
            kv, b = s // BLOCKS, s % BLOCKS
            return o[:, 2 * kv:2 * kv + 2, b * QB:(b + 1) * QB].rearrange("p j (c q) -> p c j q", c=2)

        @block.sync
        def _(sp):
            def load_tile(quad, tile, src, rows=KB, wait=True):
                if wait:
                    sp.wait_ge(w_split, 4 * quad + 2 * tile - 2)
                sp.dma_start(raw[:, tile, 0:rows, :], src).then_inc(raw_loaded[tile], 16)

            def by_rows(w):
                return w.rearrange("(k p) n -> p k n", p=P)

            def place_lags(b):
                sp.wait_ge(k_ready_d, b + 1)
                if b == 0:
                    sp.wait_ge(toep_cleared, 1)
                if b >= 2:
                    sp.wait_ge(y_ready, b - 1)
                for s in range(T):
                    for j in range(2):
                        sp.dma_start(
                            k_toep[(T - 1 - s) * GROUP:(T - s) * GROUP, b % 2, j::2, s * GROUP:],
                            k_lag[j * GROUP:(j + 1) * GROUP, :, 0:T - s, :].rearrange("q r t c -> q r (t c)"),
                        ).then_inc(toep_placed, 16)

            sp.dma_start(row["lam_re"][:], lam_re.rearrange("o (r j) n -> (o r) (j n)", j=2)).then_inc(rows_loaded, 16)
            sp.dma_start(row["lam_im"][:], lam_im.rearrange("o (r j) n -> (o r) (j n)", j=2)).then_inc(rows_loaded, 16)
            sp.dma_start(dt_log[:], log_dt.rearrange("o (r j) -> (o r) j", j=2)).then_inc(rows_loaded, 16)
            xv = x.rearrange("o (c s) d -> (o c) s d", s=T)
            mv = meta_tokens.rearrange("(c s) d -> c s d", s=T)
            for i in range(4):
                sp.dma_start(xt[META // T:C, 2 * i:2 * i + 2, :], xv[:, 2 * i:2 * i + 2, :]).then_inc(x_loaded[i], 16)
                sp.dma_start(xt[0:META // T, 2 * i:2 * i + 2, :], mv[:, 2 * i:2 * i + 2, :]).then_inc(x_loaded[i], 16)
            for k, w in (("b_re", b_re), ("b_im", b_im)):
                sp.dma_start(braw[k][:], w.rearrange("o (r j) n q -> (o r) (j n q)", j=2)).then_inc(bc_loaded, 16)
            for k, w in (("c_re", c_re), ("c_im", c_im)):
                for j in range(2):
                    sp.dma_start(braw[k][:].rearrange("r (q j n) -> r q j n", q=GROUP, j=2)[:, :, j, :],
                                 w.rearrange("o (r j) q n -> (o r) j q n", j=2)[:, j]).then_inc(bc_loaded, 16)
            sp.dma_start(gain_row[:], ln_mix[0:1, :].to_broadcast([C, D])).then_inc(consts_loaded, 16)
            for j in range(2):
                sp.dma_start(d_diag[j * GROUP:(j + 1) * GROUP],
                             ssm_d.rearrange("o (r j q) -> o j r q", j=2, q=GROUP)[:, j].to_broadcast([GROUP, PAIRS, GROUP])).then_inc(consts_loaded, 16)
            sp.dma_start(sink_row[:], sinks[0:1, :].to_broadcast([P, HEADS])).then_inc(consts_loaded, 16)
            for name, v, n in (("ln_ffn0", ln_ffn[0], KB), ("ln_mix1", ln_mix[1], KB), ("ln_ffn1", ln_ffn[1], KB),
                               ("ln_f", ln_f, KB), ("b_o", b_o[0], KB), ("b_qkv", b_qkv[0], 12)):
                sp.dma_start(vecs_row[VEC[name]:VEC[name] + n, :], v.rearrange("(k p) -> k p", p=P)).then_inc(consts_loaded, 16)
            for i in range(N_GLU):
                if i == 1:
                    place_lags(0)
                    for b in range(BATCHES):
                        if b + 1 < BATCHES:
                            place_lags(b + 1)
                load_tile(i, 0, by_rows(w_glu_b[0])[:, :, 2 * P * i:2 * P * (i + 1)], wait=i > 0)
                load_tile(i, 1, by_rows(w_glu_a[0])[:, :, 2 * P * i:2 * P * (i + 1)], wait=i > 0)

            def load_ffn(layer):
                with sp.Fori(0, N_UP, 1) as i:
                    load_tile(QUAD_UP[layer] + i, 0, by_rows(w_gate[layer])[:, :, bass.ds(i * (2 * P), 2 * P)])
                    load_tile(QUAD_UP[layer] + i, 1, by_rows(w_up[layer])[:, :, bass.ds(i * (2 * P), 2 * P)])
                with sp.Fori(0, N_DOWN, 1) as i:
                    for t, (k0, nk) in enumerate(DOWN_TILES):
                        load_tile(QUAD_DOWN[layer] + 2 * i + t // 2, t % 2,
                                  by_rows(w_down[layer])[:, k0:k0 + nk, bass.ds(i * (2 * P), 2 * P)], rows=nk)

            load_ffn(0)
            qkv = by_rows(w_qkv[0])
            load_tile(QUAD_KV, 0, qkv[:, :, HEADS * HD:HEADS * HD + 2 * P])
            load_tile(QUAD_KV, 1, qkv[:, :, HEADS * HD + 2 * P:HEADS * HD + 4 * P])
            for kv in range(2):
                load_tile(QUAD_Q, kv, qkv[:, :, 2 * P * kv:2 * P * (kv + 1)])
            sp.wait_ge(kv_ready, 2)
            sp.dma_start(k_t[0:HD, :, 1, :], k_t[HD:P, :, 0, :]).then_inc(keys_swapped, 16)
            sp.dma_start(k_t[HD:P, :, 1, :], k_t[0:HD, :, 0, :]).then_inc(keys_swapped, 16)
            for kv in range(2, KV_HEADS):
                load_tile(QUAD_Q + kv // 2, kv % 2, qkv[:, :, 2 * P * kv:2 * P * (kv + 1)])
            for i in range(4):
                load_tile(QUAD_WO + i // 2, i % 2, by_rows(w_o[0])[:, :, 2 * P * i:2 * P * (i + 1)])
            load_ffn(1)
            for j in range(4):
                sp.wait_ge(out_copied, j + 1)
                sp.dma_start(out[0, j * P:(j + 1) * P, :], out_row[:, j, :]).then_inc(out_stored, 16)
            sp.wait_ge(out_stored, 64)

        @block.gpsimd
        def _(pool):
            steps = [0]

            def step(ins):
                ins.then_inc(pool_step, 1)
                steps[0] += 1
                pool.wait_ge(pool_step, steps[0])

            nc.gpsimd.memset(ones[:], 1.0)
            nc.gpsimd.memset(neg_half[:], -0.5)
            nc.gpsimd.memset(two[:], 2.0)
            nc.gpsimd.memset(bbar_pair[:], 0.0).then_inc(pairs_cleared, 1)
            step(nc.gpsimd.memset(ident[:], 0.0))
            nc.gpsimd.affine_select(out=ident[:], in_=ident[:], compare_op=ALU.not_equal, fill=1.0, base=0,
                                    pattern=[[-1, P]], channel_multiplier=1).then_inc(consts_made, 1)
            pool.wait_ge(dt_arg, 1)
            nc.gpsimd.tensor_tensor(dt_row[:], two[:, 0:2], dt_log2[:], ALU.pow).then_inc(dt_ready, 1)
            pool.wait_ge(mag_arg, 1)
            nc.gpsimd.tensor_tensor(row["mag"][:], two[:], row["decay_arg"][:], ALU.pow).then_inc(mag_ready, 1)
            pool.wait_ge(mean_ready0, 1)
            nc.gpsimd.tensor_tensor(rstd[0:C, 0:T], mean_sq[0:C, 0:T], neg_half[0:C, 0:T], ALU.pow).then_inc(rstd0, 1)

            for b in range(BATCHES):
                pr = slice(b * PB, (b + 1) * PB)
                if b == 0:
                    pool.wait_ge(nat_copied, 4)
                    nc.gpsimd.memset(k_toep[:], 0.0).then_inc(toep_cleared, 1)
                    pool.wait_ge(turns_ready, 1)
                if b >= 2:
                    pool.wait_ge(state_ready, b - 1)
                shape = [P, PB, TA, TA]
                fr, fi = (fine[:, i, pr, 0:TA].unsqueeze(2).to_broadcast(shape) for i in range(2))
                gr, gi = (coarse[:, i, pr, 0:TA].unsqueeze(3).to_broadcast(shape) for i in range(2))
                tr, ti = (turn[:, b % 2, i, :, 0:TA * TA].rearrange("p r (a f) -> p r a f", f=TA) for i in range(2))
                nc.gpsimd.tensor_tensor(tr, gr, fr, ALU.mult)
                nc.gpsimd.tensor_tensor(turn_t[:, 0], gi, fi, ALU.mult)
                nc.gpsimd.tensor_tensor(ti, gr, fi, ALU.mult)
                step(nc.gpsimd.tensor_tensor(turn_t[:, 1], gi, fr, ALU.mult))
                nc.gpsimd.tensor_copy(turn[:, b % 2, 0, :, TA * TA], coarse[:, 0, pr, TA])
                nc.gpsimd.tensor_copy(turn[:, b % 2, 1, :, TA * TA], coarse[:, 1, pr, TA])
                nc.gpsimd.tensor_tensor(tr, tr, turn_t[:, 0], ALU.subtract)
                nc.gpsimd.tensor_tensor(ti, ti, turn_t[:, 1], ALU.add).then_inc(turn_ready, 1)

                if b == 0:
                    pool.wait_ge(nat_ready, 1)
                if b >= 3:
                    pool.wait_ge(y_ready, b - 2)
                rr, ri = read[:, b % 3, 0], read[:, b % 3, 1]
                cr = nat["c_re"][:, pr, :].unsqueeze(2)
                ci = nat["neg_c_im"][:, pr, :].unsqueeze(2)
                shape = [P, PB, T, GROUP]
                lr = powr[:, 0, 1:T + 1, pr].rearrange("p t r -> p r t").unsqueeze(3).to_broadcast(shape)
                li = powr[:, 1, 1:T + 1, pr].rearrange("p t r -> p r t").unsqueeze(3).to_broadcast(shape)
                crb, cib = cr.to_broadcast(shape), ci.to_broadcast(shape)
                nc.gpsimd.tensor_copy(rr[:, :, 0, :], nat["c_re"][:, pr, :])
                nc.gpsimd.tensor_copy(ri[:, :, 0, :], nat["neg_c_im"][:, pr, :])
                nc.gpsimd.tensor_tensor(rr[:, :, 1:, :], crb, lr, ALU.mult)
                step(nc.gpsimd.tensor_tensor(read_t[:], cib, li, ALU.mult))
                nc.gpsimd.tensor_tensor(rr[:, :, 1:, :], rr[:, :, 1:, :], read_t[:], ALU.add)
                step(nc.gpsimd.tensor_tensor(ri[:, :, 1:, :], cib, lr, ALU.mult))
                step(nc.gpsimd.tensor_tensor(read_t[:], crb, li, ALU.mult))
                nc.gpsimd.tensor_tensor(ri[:, :, 1:, :], ri[:, :, 1:, :], read_t[:], ALU.subtract).then_inc(read_ready, 1)

            def norm(index, n):
                tt, nt, _ = norm_tiles(n)
                pool.wait_ge(mean_taken, index + 1)
                nc.gpsimd.tensor_tensor(rstd[0:tt, 0:nt], mean_sq[0:tt, 0:nt], neg_half[0:tt, 0:nt],
                                        ALU.pow).then_inc(rstd_ready, 1)

            def feed_forward(layer, n, it0):
                a, e = (0, L) if n == L else (META, L)
                with pool.Fori(0, N_UP, 1) as i:
                    for j in range(2):
                        pool.wait_ge(gate_ready, 2 * i + (2 * it0 + j + 1))
                        nc.gpsimd.tensor_tensor(gate[:, j, a:e], gate[:, j, a:e], rstd_row[:, a:e], ALU.mult).then_inc(gate_scaled, 1)

            norm(0, L)
            feed_forward(0, L, N_GLU)
            norm(1, L)
            pool.wait_ge(w_used, 4 * QUAD_KV)
            step(nc.gpsimd.memset(v_meta_t[:], 0.0))
            pool.wait_ge(kv_ready, 4)
            for i in range(4):
                ins = nc.gpsimd.tensor_copy(v_meta_t[:, :, i, i * META:(i + 1) * META], v_t[:, :, 0:META])
            ins.then_inc(v_meta_ready, 1)
            norm(2, SEQ)
            feed_forward(1, SEQ, N_GLU + N_UP)
            norm(3, SEQ)

        @block.scalar
        def _(act):
            def round_weights(quad, off, wait=True):
                quad, off = quad + off // 4, off % 4
                slot, j = off // 2, off % 2
                act.wait_ge(raw_loaded[slot], 16 * (quad + 1))
                if wait:
                    act.wait_ge(w_used, 4 * quad + off - 1)
                nc.scalar.copy(w_high[:, j], raw[:, slot, :, j * P:(j + 1) * P]).then_inc(w_rounded, 1)

            act.wait_ge(angle_ready, 1)
            nc.scalar.activation(row["sin"][:], row["angle"][:], ACT.Sin)
            nc.scalar.activation(row["cos"][:], row["abs_angle"][:], ACT.Sin).then_inc(trig_ready, 1)
            for s in range(T):
                if s % 2 == 0:
                    act.wait_ge(x_loaded[s // 2], 32)
                if s > 0:
                    act.wait_ge(x_squared, s)
                nc.scalar.activation(banks[0:C, 6:8, :], xt[:, s, :].rearrange("c (h n) -> c h n", h=2), ACT.Square, accum_out=mean_sq[0:C, s:s + 1]).then_inc(x_squared, 1)
            res_v = residual[:].rearrange("p k (c s) -> p k c s", s=T)
            for s in range(T):
                act.wait_ge(res_t, s + 1)
                b0 = 2 * (s % 2)
                nc.scalar.copy(res_v[:, :, :, s].rearrange("p (h k) c -> p h k c", h=2),
                               banks[:, b0:b0 + 2, 0:4 * C].rearrange("p h (k c) -> p h k c", k=4)).then_inc(res_copied, 1)
            act.wait_ge(vecs_t, 1)
            nc.scalar.copy(vecs[:], banks[:, 4, 0:VECS]).then_inc(vecs_ready, 1)
            act.wait_ge(vecs_ready, 1)
            nc.scalar.mul(q_bias[:], vecs[:, VEC["b_qkv"]:VEC["b_qkv"] + KB], SCALE).then_inc(act_step, 1)
            for i, (k, s) in enumerate((("b_re", 1.0), ("b_im", 1.0), ("c_re", 1.0), ("neg_c_im", -1.0))):
                act.wait_ge(nat_tr, i + 1)
                nc.scalar.mul(nat[k][:].rearrange("p r q -> p q r"),
                              banks[:, 4 + i % 2, 0:GROUP * PAIRS].rearrange("p (q r) -> p q r", q=GROUP), s).then_inc(nat_copied, 1)
            for i in range(8):
                act.wait_ge(u_tr, i + 1)
                b0 = 2 * (i % 2)
                nc.scalar.copy(u_state[:, 8 * i:8 * i + 8, :].rearrange("p (h g) c -> p h (g c)", h=2),
                               banks[:, b0:b0 + 2, 0:4 * C]).then_inc(u_copied, 1)

            def front(b):
                act.wait_ge(inj_tr, b + 1)
                if b >= 1:
                    act.wait_ge(v_ready, b)
                nc.scalar.copy(inj_T[:].rearrange("p r i n -> p (r i n)").rearrange("p (h n) -> p h n", h=2),
                               banks[:, 0:2, :]).then_inc(inj_copied, 1)

            def lags(b):
                act.wait_ge(k_ready, b + 1)
                if b >= 1:
                    act.wait_ge(toep_placed, 16 * 2 * T * b)
                nc.scalar.copy(k_lag[:].rearrange("q r t c -> q (r t c)"), banks[0:2 * GROUP, 4 + b % 2, :]).then_inc(k_copied, 1)

            def gelu(b):
                act.wait_ge(y_ready, b + 1)
                if b >= 2:
                    act.wait_ge(y_stored, 16 * (b - 1))
                nc.scalar.activation(y_act[:, b % 2].rearrange("p (r j) c -> p j r c", j=2),
                                     banks[:, 6:8, 0:4 * C].rearrange("p j (r c) -> p j r c", r=PB),
                                     ACT.Gelu_apprx_tanh).then_inc(gelu_ready, 1)

            def store_outputs(b):
                act.wait_ge(gelu_ready, b + 1)
                nc.scalar.dma_start(y_dram[b].rearrange("s q g c -> (s q) (g c)"),
                                    y_act[:, b % 2].rearrange("p g c -> p (g c)")).then_inc(y_stored, 16)

            def load_outputs(b):
                act.wait_ge(y_stored, 16 * (b + 1))
                if b >= 2:
                    act.wait_ge(gt_split, b - 1)
                for g in range(GB):
                    nc.scalar.dma_start(y_feat[g * GROUP:(g + 1) * GROUP, b % 2],
                                        y_dram[b, :, :, g, :].rearrange("s q c -> q s c")).then_inc(y_placed, 16)

            def round_input(b):
                act.wait_ge(y_placed, 16 * GB * (b + 1))
                nc.scalar.copy(glu_high[:, b], y_feat[:, b % 2].rearrange("p s c -> p (s c)")).then_inc(gt_rounded, 1)

            act.wait_ge(pairs_cleared, 1)
            act.wait_ge(nat_ready, 1)
            for j in range(2):
                for i, part in enumerate(("b_re", "b_im")):
                    ins = nc.scalar.copy(bbar_pair[j * STATE:(j + 1) * STATE, i, :, j * GROUP:(j + 1) * GROUP],
                                         nat[part][j * STATE:(j + 1) * STATE])
            ins.then_inc(bbar_placed, 1)
            front(0)
            lags(0)
            for b in range(BATCHES):
                if b + 1 < BATCHES:
                    front(b + 1)
                    if b >= 1:
                        load_outputs(b - 1)
                    lags(b + 1)
                else:
                    load_outputs(b - 1)
                if b >= 1:
                    round_input(b - 1)
                gelu(b)
                store_outputs(b)
            load_outputs(BATCHES - 1)
            round_input(BATCHES - 1)
            round_weights(0, 0, wait=False)
            round_weights(0, 1, wait=False)

            def updated(k, m, n, gain):
                act.wait_ge(added, k + 1)
                act.wait_ge(sq_added, k)
                a, e = (0, L) if n == L else (META, L)
                if gain != "ln_f":
                    nc.scalar.mul(rows(x_high, m, a, e), rows(residual, m, a, e), gain_of(gain, m)).then_inc(x_rounded, 1)
                nc.scalar.activation(square[:, a:e], rows(residual, m, a, e), ACT.Square).then_inc(squared, 1)

            def gated(quad, it, func, n):
                for j in range(2):
                    act.wait_ge(w_used, 4 * quad + j + 1)
                    if it > 0:
                        act.wait_ge(up_taken, 2 * it - 1 + j)
                    nc.scalar.activation(cols(gate[:, j], n), bank_view(2 * j, n), func).then_inc(gate_ready, 1)
                    round_weights(quad, 2 + j)
                for j in range(2):
                    round_weights(quad, 4 + j)

            for i in range(N_GLU):
                gated(QUAD_GLU + i, i, ACT.Sigmoid, L)
                for j in range(2):
                    updated(2 * i + j, 2 * i + j, L, "ln_ffn0")

            def spread_norm(index, n):
                act.wait_ge(rstd_spread, index + 1)
                nc.scalar.copy(cols(rstd_row[:], n), rstd_banks(n)).then_inc(rstd_copied, 1)

            def feed_forward(layer, n, it0, adds0, index, gain):
                a, e = (0, L) if n == L else (META, L)

                def up(i, first=False):
                    quad = QUAD_UP[layer] + i
                    for j in range(2):
                        round_weights(quad, 2 + j)
                        if first and j == 0:
                            spread_norm(index, n)
                        act.wait_ge(pre_ready, 2 * i + (2 * N_UP * layer + j + 1))
                        nc.scalar.activation(gate[:, j, a:e], gate[:, j, a:e], ACT.Silu).then_inc(gate_ready, 1)
                    for j in range(2):
                        round_weights(quad, 4 + j)
                        act.wait_ge(up_taken, 2 * i + (2 * it0 + j + 1))
                        nc.scalar.copy(rows(a_high, 2 * i + j, a, e), prod[:, j, a:e]).then_inc(a_rounded, 1)

                def down(i, last):
                    quad = QUAD_DOWN[layer] + 2 * i
                    for off in range(6):
                        round_weights(quad, 2 + off)
                    for j in range(2):
                        if not last:
                            round_weights(quad, 8 + j)
                        updated(2 * i + (adds0 + j), 2 * i + j, n, gain)

                up(0, first=True)
                with act.Fori(1, N_UP, 1) as i:
                    up(i)
                if layer == 0:
                    with act.Fori(0, N_DOWN, 1) as i:
                        down(i, False)
                else:
                    with act.Fori(0, N_DOWN - 1, 1) as i:
                        down(i, False)
                    down(N_DOWN - 1, True)

            feed_forward(0, L, N_GLU, KB, 0, "ln_mix1")
            for off in range(4):
                round_weights(QUAD_KV, 2 + off)
                if off == 0:
                    spread_norm(1, L)
                act.wait_ge(kv_scaled, off + 1)
                dst = k_t[:, off, 0, :] if off < 2 else v_t[:, off - 2, :]
                col = VEC["b_qkv"] + HEADS * HD // P + off
                nc.scalar.activation(dst, (gate if off < 2 else prod)[:, off % 2, :], ACT.Identity,
                                     bias=vecs[:, col:col + 1]).then_inc(kv_ready, 1)

            def query_block(i):
                kv, j = i // 2, i % 2
                act.wait_ge(q_scaled, i + 1)
                if kv >= 2:
                    act.wait_ge(scores_ready, (kv - 1) * BLOCKS)
                nc.scalar.activation(q_t[:, kv % 2, j, :], gate[:, j, 0:SEQ], ACT.Identity, scale=SCALE,
                                     bias=q_bias[:, i:i + 1]).then_inc(q_ready, 1)

            def exponentials(s):
                b = s % BLOCKS
                act.wait_ge(shifted, s + 1)
                for h, c in HALVES:
                    w = META + CHUNK if b == 0 and c == 0 else WIN
                    nc.scalar.activation(prob_e[:, h, c, 0:w], scores_of(s)[:, h, c, 0:w], ACT.Exp,
                                         bias=neg_max[:, s % 2, h, c:c + 1], accum_out=denom[:, s % 2, h, c:c + 1])
                nc.scalar.activation(sink_exp[:, s % 2], sink_exp[:, s % 2], ACT.Exp).then_inc(prob_ready, 1)

            def prob_transposed(s):
                act.wait_ge(prob_tr, s + 1)
                if s >= 2:
                    act.wait_ge(o_ready, s - 1)
                nc.scalar.copy(prob_tb[:, s % 2].rearrange("p i q -> p (i q)"), banks[:, 6, :])
                nc.scalar.copy(prob_tm[:, s % 2], meta_of(s)).then_inc(prob_t_ready, 1)

            def out_high(s):
                act.wait_ge(o_ready, s + 1)
                nc.scalar.copy(heads_out(o_high, s), banks[:, 7, 0:2 * P].rearrange("p (c j q) -> p c j q", c=2, j=2)).then_inc(o_rounded, 1)

            for i in range(2):
                round_weights(QUAD_Q, 2 + i)
                query_block(i)
            act.wait_ge(v_tr, 1)
            nc.scalar.copy(v_win[:].rearrange("p w n -> p (w n)")[:, 0:4 * 256].rearrange("p (b n) -> p b n", b=2), banks[:, 4:6, :])
            nc.scalar.copy(v_win[:, 4:6, :].rearrange("p w n -> p (w n)"), banks[:, 6, :])
            nc.scalar.copy(v_win[:, 6, :], banks[:, 7, 0:256])
            nc.scalar.copy(v_meta[:].rearrange("p i n -> p (i n)").rearrange("p (b n) -> p b n", b=2),
                           banks[0:4 * META, 2:4, :]).then_inc(v_rows_ready, 1)
            for s in range(STEPS + 2):
                if 1 <= s < STEPS + 1:
                    prob_transposed(s - 1)
                if s < STEPS:
                    exponentials(s)
                if s >= 2:
                    out_high(s - 2)
                if s in QUERY_STEPS:
                    round_weights(QUAD_Q, 4 + s // 2)
                    query_block(2 + s // 2)
            for m in range(KB):
                round_weights(QUAD_WO, 2 + m)
                updated(2 * KB + m, m, SEQ, "ln_ffn1")
            feed_forward(1, SEQ, N_GLU + N_UP, 3 * KB, 2, "ln_f")
            act.wait_ge(rstd_ready, 4)
            for j in range(4):
                for h in range(2):
                    act.wait_ge(out_tr, 2 * j + h + 1)
                    ins = nc.scalar.mul(out_row[:, j, h * 512:(h + 1) * 512], banks[:, (2 * j + h) % 8, :], rstd[:, j:j + 1])
                ins.then_inc(out_copied, 1)

        @block.vector
        def _(dve):
            steps = [0]

            def mark(ins):
                ins.then_inc(dve_step, 1)
                steps[0] += 1

            def step(ins):
                mark(ins)
                dve.wait_ge(dve_step, steps[0])

            def split_weights(quad, off):
                quad, off = quad + off // 4, off % 4
                slot, j = off // 2, off % 2
                dve.wait_ge(w_rounded, 4 * quad + (off + 1))
                nc.vector.tensor_tensor(w_low[:, j], raw[:, slot, :, j * P:(j + 1) * P], w_high[:, j],
                                        ALU.subtract).then_inc(w_split, 1)

            TT, TS, STT = nc.vector.tensor_tensor, nc.vector.tensor_scalar, nc.vector.scalar_tensor_tensor
            r = {k: v[:] for k, v in row.items()}
            dve.wait_ge(rows_loaded, 48)
            TS(dt_log2[:], dt_log[:], LOG2E, None, ALU.mult).then_inc(dt_arg, 1)
            step(TS(r["lam_re"], r["lam_re"], -1e-4, None, ALU.min))
            dve.wait_ge(dt_ready, 1)
            for j in range(2):
                h = slice(j * STATE, (j + 1) * STATE)
                TS(r["decay_arg"][:, h], r["lam_re"][:, h], dt_row[:, j:j + 1], LOG2E, ALU.mult, ALU.mult)
                mark(TS(r["angle"][:, h], r["lam_im"][:, h], dt_row[:, j:j + 1], None, ALU.mult))
            dve.wait_ge(dve_step, steps[0])
            TS(r["turns"], r["angle"], 1.0 / (2 * math.pi), ROUND, ALU.mult, ALU.add).then_inc(mag_arg, 1)
            dve.wait_ge(mag_arg, 1)
            step(TS(r["turns"], r["turns"], ROUND, None, ALU.subtract))
            step(STT(r["angle"], r["turns"], -TWO_PI_HIGH, r["angle"], ALU.mult, ALU.add))
            step(STT(r["angle"], r["turns"], -TWO_PI_LOW, r["angle"], ALU.mult, ALU.add))
            step(TS(r["angle"], r["angle"], PI_BELOW, -PI_BELOW, ALU.min, ALU.max))
            step(TS(r["abs_angle"], r["angle"], -1.0, None, ALU.mult))
            step(TT(r["abs_angle"], r["angle"], r["abs_angle"], ALU.max))
            TS(r["abs_angle"], r["abs_angle"], -1.0, math.pi / 2, ALU.mult, ALU.add).then_inc(angle_ready, 1)
            TT(r["t0"], r["lam_re"], r["lam_re"], ALU.mult)
            step(TT(r["t1"], r["lam_im"], r["lam_im"], ALU.mult))
            step(TT(r["t0"], r["t0"], r["t1"], ALU.add))
            nc.vector.reciprocal(r["t3"], r["t0"])
            dve.wait_ge(trig_ready, 1)
            dve.wait_ge(mag_ready, 1)
            TT(r["lam_bar_re"], r["mag"], r["cos"], ALU.mult)
            step(TT(r["lam_bar_im"], r["mag"], r["sin"], ALU.mult))
            step(TS(r["lr1"], r["lam_bar_re"], 1.0, None, ALU.subtract))
            TT(r["t0"], r["lr1"], r["lam_re"], ALU.mult)
            step(TT(r["t1"], r["lam_bar_im"], r["lam_im"], ALU.mult))
            step(TT(r["t0"], r["t0"], r["t1"], ALU.add))
            TT(r["w_re"], r["t0"], r["t3"], ALU.mult)
            TT(r["t2"], r["lam_bar_im"], r["lam_re"], ALU.mult)
            step(TT(r["t1"], r["lr1"], r["lam_im"], ALU.mult))
            step(TT(r["t2"], r["t2"], r["t1"], ALU.subtract))
            TT(r["w_im"], r["t2"], r["t3"], ALU.mult)
            TT(r["decay"], r["mag"], r["mag"], ALU.mult)
            step(TT(r["turn_re"], r["cos"], r["cos"], ALU.mult))
            step(TT(r["t1"], r["sin"], r["sin"], ALU.mult))
            TT(r["turn_im"], r["cos"], r["sin"], ALU.mult)
            step(TT(r["turn_re"], r["turn_re"], r["t1"], ALU.subtract))
            step(TS(r["turn_im"], r["turn_im"], 2.0, None, ALU.mult))
            for i in range(2):
                TT(r["t0"], r["turn_re"], r["turn_re"], ALU.mult)
                TT(r["t1"], r["turn_im"], r["turn_im"], ALU.mult)
                step(TT(r["t2"], r["turn_re"], r["turn_im"], ALU.mult))
                step(TT(r["decay"], r["decay"], r["decay"], ALU.mult))
                TT(r["turn_re"], r["t0"], r["t1"], ALU.subtract)
                ins = TS(r["turn_im"], r["t2"], 2.0, None, ALU.mult)
                if i == 0:
                    step(ins)
                else:
                    ins.then_inc(rows_ready, 1)
            dve.wait_ge(rows_t, 1)
            nc.vector.tensor_copy(lam_t[:], banks[:, 6, 0:len(ROW_NAMES) * PAIRS].rearrange("p (k r) -> p k r", r=PAIRS)).then_inc(rows_copied, 1)
            dve.wait_ge(rows_copied, 1)

            def cmul(dr, di, ar, ai, br, bi, t0, t1):
                TT(dr, ar, br, ALU.mult)
                TT(t0, ai, bi, ALU.mult)
                TT(di, ar, bi, ALU.mult)
                step(TT(t1, ai, br, ALU.mult))
                TT(dr, dr, t0, ALU.subtract)
                step(TT(di, di, t1, ALU.add))

            nc.vector.memset(powr[:, 0, 0], 1.0)
            nc.vector.memset(powr[:, 1, 0], 0.0)
            step(nc.vector.tensor_copy(powr[:, :, 1], lam_t[:, 0:2]))
            k = 1
            while k < T:
                s = [P, k, PAIRS]
                cmul(powr[:, 0, k + 1:2 * k + 1], powr[:, 1, k + 1:2 * k + 1], powr[:, 0, 1:k + 1], powr[:, 1, 1:k + 1],
                     powr[:, 0, k:k + 1].to_broadcast(s), powr[:, 1, k:k + 1].to_broadcast(s), pow_t[:, 0, 0:k], pow_t[:, 1, 0:k])
                k *= 2
            pow_v = pow_t[:].rearrange("p i k r -> p i (k r)").rearrange("p i (r k) -> p i r k", k=4)
            for tab, first in ((fine, lam_t[:, 5:7, :]), (coarse, fine[:, :, :, TA])):
                nc.vector.memset(tab[:, 0, :, 0:1], 1.0)
                nc.vector.memset(tab[:, 1, :, 0:1], 0.0)
                step(nc.vector.tensor_copy(tab[:, :, :, 1], first))
                k = 1
                while k < TA:
                    s = [P, PAIRS, k]
                    cmul(tab[:, 0, :, k + 1:2 * k + 1], tab[:, 1, :, k + 1:2 * k + 1], tab[:, 0, :, 1:k + 1], tab[:, 1, :, 1:k + 1],
                         tab[:, 0, :, k:k + 1].to_broadcast(s), tab[:, 1, :, k:k + 1].to_broadcast(s),
                         pow_v[:, 0, :, 0:k], pow_v[:, 1, :, 0:k])
                    k *= 2
            nc.vector.memset(pow_t[:, 0, 0, 0:1], 0.0).then_inc(turns_ready, 1)
            dve.wait_ge(nat_copied, 4)
            wr = lam_t[:, 2].unsqueeze(2).to_broadcast([P, PAIRS, GROUP])
            wi = lam_t[:, 3].unsqueeze(2).to_broadcast([P, PAIRS, GROUP])
            nat_t = read_t[:].rearrange("p r s q -> p (r s q)").rearrange("p (r q) -> p r q", q=GROUP)
            step(TT(nat_t, nat["b_re"][:], wi, ALU.mult))
            TT(nat["b_re"][:], nat["b_re"][:], wr, ALU.mult)
            sc = inj_t[:].rearrange("p r s q -> p (r s q)").rearrange("p (r q) -> p r q", q=GROUP)
            step(TT(sc, nat["b_im"][:], wi, ALU.mult))
            step(TT(nat["b_re"][:], nat["b_re"][:], sc, ALU.subtract))
            step(TT(nat["b_im"][:], nat["b_im"][:], wr, ALU.mult))
            TT(nat["b_im"][:], nat["b_im"][:], nat_t, ALU.add).then_inc(nat_ready, 1)
            dve.wait_ge(nat_ready, 1)

            dve.wait_ge(x_squared, T)
            TS(mean_sq[0:C, 0:T], mean_sq[0:C, 0:T], 1.0 / D, EPS, ALU.mult, ALU.add).then_inc(mean_ready0, 1)

            def make_injection(b):
                pr = slice(b * PB, (b + 1) * PB)
                shape = [P, PB, T, GROUP]
                lr = powr[:, 0, 0:T, pr].rearrange("p t r -> p r t").unsqueeze(3).to_broadcast(shape)
                li = powr[:, 1, 0:T, pr].rearrange("p t r -> p r t").unsqueeze(3).to_broadcast(shape)
                br = nat["b_re"][:, pr, :].unsqueeze(2).to_broadcast(shape)
                bi = nat["b_im"][:, pr, :].unsqueeze(2).to_broadcast(shape)
                if b >= 1:
                    dve.wait_ge(inj_tr, b)
                TT(inj[:, 0], br, lr, ALU.mult)
                step(TT(inj_t[:], bi, li, ALU.mult))
                TT(inj[:, 0], inj[:, 0], inj_t[:], ALU.subtract)
                step(TT(inj[:, 1], bi, lr, ALU.mult))
                step(TT(inj_t[:], br, li, ALU.mult))
                TT(inj[:, 1], inj[:, 1], inj_t[:], ALU.add).then_inc(inj_ready, 1)

            make_injection(0)
            dve.wait_ge(consts_loaded, 10 * 16)
            dve.wait_ge(consts_made, 1)
            step(TT(diag_mask[:], ident[0:2 * GROUP, 0:GROUP], ident[0:2 * GROUP, GROUP:2 * GROUP], ALU.add))
            step(TT(d_diag[:], d_diag[:], diag_mask[:].unsqueeze(1).to_broadcast([2 * GROUP, PAIRS, GROUP]), ALU.mult))
            dve.wait_ge(rstd0, 1)
            for i in range(4):
                if i >= 2:
                    dve.wait_ge(u_tr, 2 * i - 2)
                for s in range(T):
                    ins = STT(u_row[:, i % 2, :, T - 1 - s, :], xt[:, s, i * 256:(i + 1) * 256].rearrange("c (g q) -> c g q", q=GROUP),
                              rstd[0:C, s:s + 1], gain_row[:, i * 256:(i + 1) * 256].rearrange("c (g q) -> c g q", q=GROUP),
                              ALU.mult, ALU.mult)
                ins.then_inc(u_normed, 1)

            nc.vector.memset(decay_row[:], 0.0)
            flat = lambda ap: ap.rearrange("p r c -> p (r c)")
            def skip_joins(b):
                dve.wait_ge(k_copied, b + 1)
                TT(k_lag[:, :, 0, :], k_lag[:, :, 0, :], d_diag[:, b * PB:(b + 1) * PB, :], ALU.add).then_inc(k_ready_d, 1)

            def split_input(b):
                dve.wait_ge(gt_rounded, b + 1)
                TT(glu_low[:, b], y_feat[:, b % 2].rearrange("p s c -> p (s c)"), glu_high[:, b], ALU.subtract).then_inc(gt_split, 1)

            skip_joins(0)
            make_injection(1)
            for b in range(BATCHES):
                pr = slice(b * PB, (b + 1) * PB)
                step(nc.vector.tensor_copy(decay_row[:, :, 1:], lam_t[:, 4, pr].unsqueeze(2).to_broadcast([P, PB, CS - 1])))
                tr, ti = turn[:, b % 2, 0], turn[:, b % 2, 1]
                vr = banks[:, 2, 0:PB * CS].rearrange("p (r c) -> p r c", r=PB)
                vi = banks[:, 3, 0:PB * CS].rearrange("p (r c) -> p r c", r=PB)
                dve.wait_ge(turn_ready, b + 1)
                dve.wait_ge(v_ready, b + 1)
                TT(z[:, 0], vr, tr, ALU.mult)
                TT(zt[:, 0], vi, ti, ALU.mult)
                TT(z[:, 1], vi, tr, ALU.mult)
                TT(zt[:, 1], vr, ti, ALU.mult).then_inc(v_taken, 1)
                dve.wait_ge(v_taken, b + 1)
                TT(z[:, 0], z[:, 0], zt[:, 0], ALU.add)
                step(TT(z[:, 1], z[:, 1], zt[:, 1], ALU.subtract))
                for i in range(2):
                    ins = nc.vector.tensor_tensor_scan(flat(zs[:, i]), flat(decay_row[:]), flat(z[:, i]), 0.0, ALU.mult, ALU.add)
                step(ins)
                TT(zt[:, 0], zs[:, 0], tr, ALU.mult)
                TT(zt[:, 1], zs[:, 1], ti, ALU.mult)
                TT(z[:, 0], zs[:, 0], ti, ALU.mult)
                step(TT(z[:, 1], zs[:, 1], tr, ALU.mult))
                if b >= 1:
                    dve.wait_ge(y_ready, b)
                TT(state[:, 0], zt[:, 0], zt[:, 1], ALU.subtract)
                TT(state[:, 1], z[:, 0], z[:, 1], ALU.add).then_inc(state_ready, 1)

                if b + 2 < BATCHES:
                    make_injection(b + 2)
                if b + 1 < BATCHES:
                    skip_joins(b + 1)
                if b >= 2:
                    split_input(b - 2)
            split_input(BATCHES - 2)
            split_input(BATCHES - 1)
            step(nc.vector.memset(sq_sum[:], 0.0))
            split_weights(0, 0)
            split_weights(0, 1)

            def updated(k, m, n, gain):
                a, e = (0, L) if n == L else (META, L)
                if gain != "ln_f":
                    dve.wait_ge(x_rounded, k + 1)
                    STT(rows(x_low, m, a, e), rows(residual, m, a, e), gain_of(gain, m), rows(x_high, m, a, e),
                        ALU.mult, ALU.subtract).then_inc(x_split, 1)
                dve.wait_ge(squared, k + 1)
                TT(sq_sum[:, a:e], sq_sum[:, a:e], square[:, a:e], ALU.add).then_inc(sq_added, 1)

            for i in range(N_GLU):
                quad = QUAD_GLU + i
                for j in range(2):
                    split_weights(quad, 2 + j)
                for j in range(2):
                    dve.wait_ge(w_used, 4 * quad + 2 + j + 1)
                    dve.wait_ge(gate_ready, 2 * i + j + 1)
                    TT(cols(prod[:, j], L), bank_view(4 + 2 * j, L), cols(gate[:, j], L), ALU.mult).then_inc(up_taken, 1)
                    dve.wait_ge(up_taken, 2 * i + j + 1)
                    res = residual[:, 2 * i + j].rearrange("p (c s) -> p s c", s=T)
                    TT(res, res, prod[:, j].rearrange("p (s c) -> p s c", s=T), ALU.add).then_inc(added, 1)
                    split_weights(quad, 4 + j)
                for j in range(2):
                    updated(2 * i + j, 2 * i + j, L, "ln_ffn0")

            def norm(index, n):
                tt, nt, _ = norm_tiles(n)
                dve.wait_ge(mean_summed, index + 1)
                TS(mean_sq[0:tt, 0:nt], banks[0:tt, 7, 0:nt], 1.0 / D, EPS, ALU.mult, ALU.add).then_inc(mean_taken, 1)
                if index == 3:
                    return
                nc.vector.memset(sq_sum[:], 0.0)
                dve.wait_ge(rstd_ready, index + 1)
                for t in range(nt):
                    ins = TS(diag[0:tt, t * tt:(t + 1) * tt], ident[0:tt, 0:tt], rstd[0:tt, t:t + 1], None, ALU.mult)
                ins.then_inc(diag_ready, 1)

            def feed_forward(layer, n, it0, adds0, index, gain):
                a, e = (0, L) if n == L else (META, L)

                def up(i, first=False):
                    quad = QUAD_UP[layer] + i
                    for j in range(2):
                        if first and j == 0:
                            split_weights(quad, 2)
                            dve.wait_ge(rstd_copied, index + 1)
                        dve.wait_ge(w_used, 4 * quad + (j + 1))
                        TT(cols(gate[:, j], n), bank_view(2 * j, n), cols(rstd_row[:], n), ALU.mult).then_inc(pre_ready, 1)
                        if not (first and j == 0):
                            split_weights(quad, 2 + j)
                    for j in range(2):
                        dve.wait_ge(w_used, 4 * quad + (2 + j + 1))
                        dve.wait_ge(gate_scaled, 2 * i + (2 * N_UP * layer + j + 1))
                        TT(cols(prod[:, j], n), bank_view(4 + 2 * j, n), cols(gate[:, j], n), ALU.mult).then_inc(up_taken, 1)
                        split_weights(quad, 4 + j)
                        dve.wait_ge(a_rounded, 2 * i + (2 * N_UP * layer + j + 1))
                        TT(rows(a_low, 2 * i + j, a, e), prod[:, j, a:e], rows(a_high, 2 * i + j, a, e),
                           ALU.subtract).then_inc(a_split, 1)

                def down(i, last):
                    quad = QUAD_DOWN[layer] + 2 * i
                    for off in range(6):
                        split_weights(quad, 2 + off)
                    for j in range(2):
                        dve.wait_ge(w_used, 4 * quad + (6 + j + 1))
                        r_m = rows(residual, 2 * i + j)
                        TT(cols(r_m, n), cols(r_m, n), bank_view(2 * j, n), ALU.add).then_inc(added, 1)
                        if not last:
                            split_weights(quad, 8 + j)
                        updated(2 * i + (adds0 + j), 2 * i + j, n, gain)

                up(0, first=True)
                with dve.Fori(1, N_UP, 1) as i:
                    up(i)
                if layer == 0:
                    with dve.Fori(0, N_DOWN, 1) as i:
                        down(i, False)
                else:
                    with dve.Fori(0, N_DOWN - 1, 1) as i:
                        down(i, False)
                    down(N_DOWN - 1, True)

            norm(0, L)
            feed_forward(0, L, N_GLU, KB, 0, "ln_mix1")
            norm(1, L)
            for j in range(2):
                TS(neg_sink[j * HD:(j + 1) * HD], sink_row[j * HD:(j + 1) * HD].rearrange("p (k j h) -> p k j h", k=KV_HEADS, j=2)[:, :, j, :],
                   -1.0, None, ALU.mult)
            for off in range(4):
                split_weights(QUAD_KV, 2 + off)
                if off == 0:
                    dve.wait_ge(rstd_copied, 2)
                dve.wait_ge(w_used, 4 * QUAD_KV + off + 1)
                TT(cols((gate if off < 2 else prod)[:, off % 2], L), bank_view(2 * off, L), cols(rstd_row[:], L), ALU.mult).then_inc(kv_scaled, 1)

            def query_block(i):
                dve.wait_ge(w_used, 4 * QUAD_Q + i + 1)
                if i < 2:
                    dve.wait_ge(kv_ready, 2)
                else:
                    dve.wait_ge(q_ready, i - 1)
                TT(gate[:, i % 2, 0:SEQ], banks[:, i % 2, :], rstd_row[:, META:], ALU.mult).then_inc(q_scaled, 1)

            def softmax_shift(s):
                kv, b = s // BLOCKS, s % BLOCKS
                dve.wait_ge(scores_ready, s + 1)
                sc = scores_of(s)
                if b == 0:
                    nc.vector.reduce_max(row_max[:, :, 0], sc[:, :, 0, 0:META + CHUNK], AX_X)
                    step(nc.vector.reduce_max(row_max[:, :, 1], sc[:, :, 1, :], AX_X))
                else:
                    step(nc.vector.reduce_max(row_max[:], sc, AX_X))
                ns = neg_sink[:, kv].unsqueeze(2).to_broadcast([P, 2, 2])
                step(STT(neg_max[:, s % 2], row_max[:], -1.0, ns, ALU.mult, ALU.min))
                TT(sink_exp[:, s % 2], neg_max[:, s % 2], ns, ALU.subtract).then_inc(shifted, 1)

            def normalize(s):
                b, i = s % BLOCKS, s % 2
                dve.wait_ge(prob_ready, s + 1)
                step(TT(denom[:, i], denom[:, i], sink_exp[:, i], ALU.add))
                step(nc.vector.reciprocal(denom[:, i], denom[:, i]))
                if s >= 2:
                    dve.wait_ge(prob_tr, s - 1)
                pb = prob_b[:, i].rearrange("p (h c) k -> p h c k", h=2)
                if b == 0:
                    for c, w in ((0, CHUNK), (1, BAND)):
                        TT(pb[:, :, c, 0:w], prob_e[:, :, c, META:META + w], denom[:, i, :, c:c + 1].to_broadcast([P, 2, w]), ALU.mult)
                else:
                    TT(pb, prob_e[:, :, :, META:], denom[:, i].unsqueeze(3).to_broadcast([P, 2, 2, BAND]), ALU.mult)
                TT(prob_m[:, i].rearrange("p (h c) k -> p h c k", h=2), prob_e[:, :, :, 0:META],
                   denom[:, i].unsqueeze(3).to_broadcast([P, 2, 2, META]), ALU.mult).then_inc(prob_scaled, 1)

            def out_low(s):
                dve.wait_ge(o_rounded, s + 1)
                TT(heads_out(o_low, s), banks[:, 7, 0:2 * P].rearrange("p (c j q) -> p c j q", c=2, j=2),
                   heads_out(o_high, s), ALU.subtract).then_inc(o_split, 1)

            for i in range(2):
                split_weights(QUAD_Q, 2 + i)
                query_block(i)
            for s in range(STEPS + 2):
                if s < STEPS:
                    softmax_shift(s)
                    normalize(s)
                if s >= 2:
                    out_low(s - 2)
                if s in QUERY_STEPS:
                    query_block(2 + s // 2)
                    split_weights(QUAD_Q, 4 + s // 2)
            for m in range(KB):
                dve.wait_ge(w_used, 4 * QUAD_WO + m + 1)
                STT(residual[:, m, META:], banks[:, m % 4, 0:SEQ], vecs[:, VEC["b_o"] + m:VEC["b_o"] + m + 1],
                    residual[:, m, META:], ALU.add, ALU.add).then_inc(added, 1)
                split_weights(QUAD_WO, 2 + m)
                updated(2 * KB + m, m, SEQ, "ln_ffn1")
            norm(2, SEQ)
            feed_forward(1, SEQ, N_GLU + N_UP, 3 * KB, 2, "ln_f")
            for kb in range(KB):
                ins = TS(scaled[:, kb, :], residual[:, kb, META:], vecs[:, VEC["ln_f"] + kb:VEC["ln_f"] + kb + 1], None, ALU.mult)
                ins.then_inc(scaled_ready, 1)
            norm(3, SEQ)

        @block.tensor
        def _(pe):
            def product(quad, off, first_k, nk, xh, xl, bank, n, start=True, stop=True, each=None, w_k=0, used=True):
                quad, off = quad + off // 4, off % 4
                j = off % 2
                pe.wait_ge(w_split, 4 * quad + (off + 1))
                parts = halves(n)
                for k in range(w_k, w_k + nk):
                    if each:
                        each(k)
                    for w, xx in ((w_high, xh), (w_high, xl), (w_low, xh)):
                        for h, (c0, cn) in enumerate(parts):
                            last_one = k == w_k + nk - 1 and w is w_low
                            base = 0 if xx is not o_high and xx is not o_low else -META
                            ins = nc.tensor.matmul(banks[:, bank + h, 0:cn], w[:, j, k, :],
                                                   xx[:, first_k + k, c0 + base:c0 + base + cn],
                                                   start=start and k == 0 and w is w_high and xx is xh,
                                                   stop=stop and last_one)
                if used:
                    ins.then_inc(w_used, 1)

            pe.wait_ge(consts_made, 1)
            for s in range(T):
                pe.wait_ge(x_loaded[s // 2], 32)
                if s >= 2:
                    pe.wait_ge(res_copied, s - 1)
                for k in range(KB):
                    ins = nc.tensor.transpose(banks[:, 2 * (s % 2) + k // 4, (k % 4) * C:(k % 4 + 1) * C],
                                              xt[:, s, k * P:(k + 1) * P], ident[0:C, 0:C])
                ins.then_inc(res_t, 1)
            pe.wait_ge(consts_loaded, 10 * 16)
            nc.tensor.transpose(banks[:, 4, 0:VECS], vecs_row[:], ident[0:VECS, 0:VECS]).then_inc(vecs_t, 1)
            pe.wait_ge(vecs_ready, 1)
            pe.wait_ge(bc_loaded, 96)
            for i, k in enumerate(("b_re", "b_im", "c_re", "c_im")):
                if i >= 2:
                    pe.wait_ge(nat_copied, i - 1)
                for q in range(GROUP):
                    if k[0] == "b":
                        src = braw[k][:].rearrange("r (n q) -> r n q", q=GROUP)[:, :, q]
                    else:
                        src = braw[k][:, q * P:(q + 1) * P]
                    ins = nc.tensor.transpose(banks[:, 4 + i % 2, q * PAIRS:(q + 1) * PAIRS], src, ident[0:PAIRS, 0:PAIRS])
                ins.then_inc(nat_tr, 1)
            pe.wait_ge(rows_ready, 1)
            for i, k in enumerate(ROW_NAMES):
                ins = nc.tensor.transpose(banks[:, 6, i * PAIRS:(i + 1) * PAIRS], row[k][:], ident[0:PAIRS, 0:PAIRS])
            ins.then_inc(rows_t, 1)
            for i in range(8):
                pe.wait_ge(u_normed, i // 2 + 1)
                if i < 2:
                    pe.wait_ge(res_copied, T)
                else:
                    pe.wait_ge(u_copied, i - 1)
                for g in range(8):
                    ins = nc.tensor.transpose(banks[:, 2 * (i % 2) + g // 4, (g % 4) * C:(g % 4 + 1) * C],
                                              u_row[:, i // 2 % 2, 8 * (i % 2) + g].rearrange("c s q -> c (s q)"),
                                              ident[0:C, 0:C])
                ins.then_inc(u_tr, 1)

            def front(b):
                pe.wait_ge(inj_ready, b + 1)
                if b == 0:
                    pe.wait_ge(u_copied, 8)
                if b >= 1:
                    pe.wait_ge(inj_copied, b)
                for r_ in range(PB):
                    for i in range(2):
                        n = 2 * r_ + i
                        ins = nc.tensor.transpose(banks[:, n // 4, (n % 4) * P:(n % 4 + 1) * P],
                                                  inj[:, i, r_].rearrange("p s q -> p (s q)"), ident[:])
                ins.then_inc(inj_tr, 1)
                pe.wait_ge(inj_copied, b + 1)
                if b >= 1:
                    pe.wait_ge(v_taken, b)
                for r_ in range(PB):
                    for j in range(2):
                        for i in range(2):
                            ins = nc.tensor.matmul(banks[j * STATE:(j + 1) * STATE, 2 + i, r_ * CS:(r_ + 1) * CS],
                                                   inj_T[:, r_, i, j * STATE:(j + 1) * STATE],
                                                   u_state[:, b * GB + 2 * r_ + j, 0:CS], start=True, stop=True)
                ins.then_inc(v_ready, 1)

            def lags(b):
                pe.wait_ge(read_ready, b + 1)
                if b == 0:
                    pe.wait_ge(bbar_placed, 1)
                if b >= 2:
                    pe.wait_ge(k_copied, b - 1)
                for r_ in range(PB):
                    for i in range(2):
                        ins = nc.tensor.matmul(banks[0:2 * GROUP, 4 + b % 2, r_ * P:(r_ + 1) * P], bbar_pair[:, i, b * PB + r_, :],
                                               read[:, b % 3, i, r_, 0:T].rearrange("p t q -> p (t q)"),
                                               start=i == 0, stop=i == 1)
                ins.then_inc(k_ready, 1)

            def outputs(b):
                pe.wait_ge(toep_placed, 16 * 2 * T * (b + 1))
                pe.wait_ge(state_ready, b + 1)
                if b >= 1:
                    pe.wait_ge(gelu_ready, b)
                for g in range(GB):
                    r_, j = g // 2, g % 2
                    bank, c0 = 6 + j, r_ * C
                    nc.tensor.matmul(banks[:, bank, c0:c0 + C], k_toep[:, b % 2, g, :], u_state[:, b * GB + g, :],
                                     start=True, stop=False)
                    for i in range(2):
                        hs = slice(j * STATE, (j + 1) * STATE)
                        ins = nc.tensor.matmul(banks[:, bank, c0 + 1:c0 + C],
                                               read[hs, b % 3, i, r_, 1:T + 1].rearrange("p t q -> p (t q)"),
                                               state[hs, i, r_, :], start=False, stop=i == 1)
                ins.then_inc(y_ready, 1)

            front(0)
            lags(0)
            for b in range(BATCHES):
                if b + 1 < BATCHES:
                    front(b + 1)
                    lags(b + 1)
                outputs(b)
            pe.wait_ge(gt_split, BATCHES)

            for i in range(N_GLU):
                for off in range(4):
                    if i > 0:
                        pe.wait_ge(gate_ready if off < 2 else up_taken, 2 * i + (off % 2 - 1))
                    product(QUAD_GLU + i, off, 0, KB, glu_high, glu_low, 2 * off, L)

            def mean(index, n):
                tt, nt, c0 = norm_tiles(n)
                pe.wait_ge(sq_added, KB * (index + 1))
                for t in range(nt):
                    ins = nc.tensor.matmul(banks[0:tt, 7, t:t + 1], sq_sum[:, c0 + t * tt:c0 + (t + 1) * tt], ones[:, 0:1],
                                           start=True, stop=True)
                ins.then_inc(mean_summed, 1)

            def spread(index, n):
                tt, nt, _ = norm_tiles(n)
                pe.wait_ge(diag_ready, index + 1)
                for t in range(nt):
                    o = rstd_banks(n)[:, t // 3, (t % 3) * tt:(t % 3 + 1) * tt] if n == L else rstd_banks(n)[:, t * tt:(t + 1) * tt]
                    ins = nc.tensor.matmul(o, ones[0:tt, :], diag[0:tt, t * tt:(t + 1) * tt], start=True, stop=True)
                ins.then_inc(rstd_spread, 1)

            def first_quad(quad, index, n, bank_free, up_free):
                for off in range(4):
                    if off < 2:
                        pe.wait_ge(*bank_free[off])
                    if off == 3:
                        pe.wait_ge(rstd_copied, index + 1)
                    if off >= 2 and up_free is not None:
                        pe.wait_ge(up_taken, up_free + off - 2)
                    product(quad, off, 0, KB, x_high, x_low, 2 * off, n,
                            each=(lambda k: pe.wait_ge(x_split, KB * index + k + 1)) if off == 0 else None)
                    if off == 0:
                        mean(index, n)
                    if off == 1:
                        spread(index, n)

            def feed_forward(layer, n, it0, adds0, index, bank_free):
                first_quad(QUAD_UP[layer], index, n, bank_free, 2 * it0 - 1 if layer == 0 else None)
                with pe.Fori(1, N_UP, 1) as i:
                    for off in range(4):
                        if off < 2:
                            pe.wait_ge(pre_ready, 2 * i + (2 * N_UP * layer + off - 1))
                        else:
                            pe.wait_ge(up_taken, 2 * i + (2 * it0 + off % 2 - 1))
                        product(QUAD_UP[layer] + i, off, 0, KB, x_high, x_low, 2 * off, n)

                def down(i):
                    q = QUAD_DOWN[layer] + 2 * i
                    for off in range(8):
                        k0, nk = DOWN_TILES[off // 2]
                        if off < 2:
                            pe.wait_ge(added, 2 * i + (adds0 - 1 + off))
                        product(q, off, k0, nk, a_high, a_low, 2 * (off % 2), n, start=off < 2, stop=off >= 6)

                pe.wait_ge(pre_ready, 2 * N_UP * (layer + 1))
                pe.wait_ge(a_split, 2 * N_UP * (layer + 1))
                with pe.Fori(0, N_DOWN, 1) as i:
                    down(i)

            feed_forward(0, L, N_GLU, KB, 0, [(gate_ready, 2 * N_GLU - 1), (gate_ready, 2 * N_GLU)])
            first_quad(QUAD_KV, 1, L, [(added, 2 * KB - 1), (added, 2 * KB)], None)

            def query_block(i):
                if i < 2:
                    pe.wait_ge(kv_scaled, 1)
                else:
                    pe.wait_ge(q_scaled, i - 1)
                product(QUAD_Q, i, 0, KB, x_high, x_low, i % 2, SEQ)

            def scores(s):
                kv, b = s // BLOCKS, s % BLOCKS
                if b == 0:
                    pe.wait_ge(q_ready, 2 * kv + 2)
                if s >= 2:
                    pe.wait_ge(prob_t_ready, s - 1)
                for h, c in HALVES:
                    hs = slice(h * HD, (h + 1) * HD)
                    keys = k_t[hs, kv // 2, 0 if kv % 2 == h else 1, :]
                    chunk = 2 * b + c
                    for j in range(2):
                        q = q_t[hs, kv % 2, j, chunk * CHUNK:(chunk + 1) * CHUNK]
                        o = scores_of(s)[j * CHUNK:(j + 1) * CHUNK, h, c]
                        if chunk < 2:
                            ins = nc.tensor.matmul(o[:, 0:META + (chunk + 1) * CHUNK], q, keys[:, 0:META + (chunk + 1) * CHUNK], start=True, stop=True)
                        else:
                            first = META + (chunk - 1) * CHUNK
                            nc.tensor.matmul(o[:, 0:META], q, keys[:, 0:META], start=True, stop=True)
                            ins = nc.tensor.matmul(o[:, META:], q, keys[:, first:first + BAND], start=True, stop=True)
                ins.then_inc(scores_ready, 1)

            def transpose_probs(s):
                pe.wait_ge(prob_scaled, s + 1)
                if s >= 1:
                    pe.wait_ge(prob_t_ready, s)
                for i, (h, c) in enumerate(HALVES):
                    w = CHUNK if s % BLOCKS == 0 and c == 0 else BAND
                    nc.tensor.transpose(banks[0:w, 6, i * P:(i + 1) * P], prob_b[:, s % 2, i, 0:w], ident[:])
                nc.tensor.transpose(meta_of(s), prob_m[:, s % 2].rearrange("p i k -> p (i k)"),
                                    ident[:]).then_inc(prob_tr, 1)

            def values(s):
                kv, b = s // BLOCKS, s % BLOCKS
                vs = slice(kv * HD, (kv + 1) * HD)
                pe.wait_ge(prob_t_ready, s + 1)
                if s >= 1:
                    pe.wait_ge(o_split, s)
                for i, (h, c) in enumerate(HALVES):
                    chunk = 2 * b + c
                    w = CHUNK if chunk == 0 else BAND
                    o = banks[h * HD:(h + 1) * HD, 7, c * P:(c + 1) * P]
                    nc.tensor.matmul(o, v_win[0:w, max(chunk - 1, 0), vs], prob_tb[0:w, s % 2, i, :], start=True, stop=False)
                    ins = nc.tensor.matmul(o, v_meta[:, i, vs], prob_tm[:, s % 2, :], start=False, stop=True)
                ins.then_inc(o_ready, 1)

            query_block(0)
            query_block(1)
            pe.wait_ge(kv_ready, 4)
            for w in range(WINDOWS):
                for t in range(2):
                    nc.tensor.transpose(banks[:, 4 + w // 2, (w % 2) * 2 * P + t * P:(w % 2) * 2 * P + (t + 1) * P],
                                        v_t[:, t, META + w * CHUNK:META + w * CHUNK + BAND], ident[:])
            pe.wait_ge(v_meta_ready, 1)
            for i in range(4):
                for t in range(2):
                    ins = nc.tensor.transpose(banks[0:4 * META, 2 + i // 2, (i % 2) * 2 * P + t * P:(i % 2) * 2 * P + (t + 1) * P],
                                              v_meta_t[:, t, i, :], ident[:])
            ins.then_inc(v_tr, 1)
            pe.wait_ge(keys_swapped, 32)
            pe.wait_ge(v_rows_ready, 1)
            for s in range(STEPS + 2):
                if s < STEPS:
                    scores(s)
                if 1 <= s < STEPS + 1:
                    transpose_probs(s - 1)
                if s >= 2:
                    values(s - 2)
                if s in QUERY_STEPS:
                    query_block(2 + s // 2)
                if s in WO_STEPS:
                    m = WO_STEPS.index(s)
                    pe.wait_ge(q_scaled, KB)
                    product(QUAD_WO, m, 0, KB - 2, o_high, o_low, m, SEQ, stop=False, used=False,
                            each=lambda k: pe.wait_ge(o_split, (k // 2 + 1) * BLOCKS))
            pe.wait_ge(o_split, STEPS)
            for m in range(KB):
                if m >= 4:
                    pe.wait_ge(added, 2 * KB + m - 3)
                if m < len(WO_STEPS):
                    product(QUAD_WO, m, 0, 2, o_high, o_low, m, SEQ, start=False, w_k=KB - 2)
                else:
                    product(QUAD_WO, m, 0, KB, o_high, o_low, m % 4, SEQ)
            feed_forward(1, SEQ, N_GLU + N_UP, 3 * KB, 2, [(added, 2 * KB + 5), (added, 2 * KB + 7)])
            pe.wait_ge(scaled_ready, KB)
            mean(3, SEQ)
            for j in range(4):
                for h in range(2):
                    i = 2 * j + h
                    if i == 0:
                        pe.wait_ge(mean_taken, 4)
                    for k in range(4):
                        ins = nc.tensor.transpose(banks[:, i, k * P:(k + 1) * P], scaled[:, 4 * h + k, j * P:(j + 1) * P], ident[:])
                    ins.then_inc(out_tr, 1)


_INS = ["x", "meta_tokens", "ln_mix", "ln_ffn", "ssm_lam_re", "ssm_lam_im", "ssm_log_dt", "ssm_b_re", "ssm_b_im",
        "ssm_c_re", "ssm_c_im", "ssm_d", "ssm_w_glu_a", "ssm_w_glu_b", "attn_w_qkv", "attn_b_qkv", "attn_sinks",
        "attn_w_o", "attn_b_o", "ffn_w_gate", "ffn_w_up", "ffn_w_down", "ln_f"]


def kernel(**inputs):
    import numpy as _np
    import concourse.bacc as _bacc
    from concourse import mybir as _mybir
    from concourse.bass_utils import run_bass_kernel_spmd as _run

    nc = _bacc.Bacc("TRN2", target_bir_lowering=False, num_devices=1)
    arrays, args = {}, []
    for name in _INS:
        a = _np.ascontiguousarray(inputs[name])
        arrays[f"in_{name}"] = a
        args.append(nc.dram_tensor(f"in_{name}", a.shape, _mybir.dt.from_np(a.dtype), kind="ExternalInput").ap())
    args.append(nc.dram_tensor("out", (1, SEQ, D), F32, kind="ExternalOutput").ap())
    trunk(nc, *args)
    r = _run(nc, [arrays], core_ids=[0])
    return r.results[0]["out"]
```

```python
import math
from contextlib import ExitStack

import concourse.bass as bass
from concourse import mybir

F32 = mybir.dt.float32
F32R = mybir.dt.float32r
ALU = mybir.AluOpType
ACT = mybir.ActivationFunctionType
AX_X = mybir.AxisListType.X

P = 128
D = 1024
KB = D // P
SEQ, META = 512, 16
L = SEQ + META
HALF = L // 2
EPS = 1e-5

GROUPS, GROUP, STATE = 64, 16, 64
T = P // GROUP
C = L // T
CS = C - 1
PAIRS = GROUPS // 2
BATCHES = 8
TA = 8
PB = PAIRS // BATCHES
GB = 2 * PB
LOG2E = 1.0 / math.log(2.0)
ROUND = 1.5 * 2.0 ** 23
TWO_PI_HIGH = 6.28125
TWO_PI_LOW = 2 * math.pi - TWO_PI_HIGH
PI_BELOW = 3.1415925
LAM_NAMES = ("lam_bar_re", "lam_bar_im", "w_re", "w_im", "decay", "turn_re", "turn_im")

HEADS, KV_HEADS, HD = 16, 4, 64
CHUNK = 64
QB = 2 * CHUNK
BLOCKS = SEQ // QB
BAND = 2 * CHUNK
WIN = META + BAND
WINDOWS = SEQ // CHUNK - 1
HALVES = ((0, 0), (0, 1), (1, 0), (1, 1))
STEPS = KV_HEADS * BLOCKS
GLU_EARLY = 6
FIRST_QUERIES = 3
QUERY_STEPS = 2 * (KB - FIRST_QUERIES)
WO_STEPS = {QUERY_STEPS + i: (i % 2, 2 * (i // 2)) for i in range(STEPS - QUERY_STEPS)}
WO_EARLY = 2 * (len(WO_STEPS) // 2)
SCALE = 1.0 / math.sqrt(HD)

FF = -(-8 * D // (3 * 256)) * 256
FB = FF // P
DOWN_TILES = ((0, 6), (6, 6), (12, 5), (17, 5))

QUAD_GLU, N_GLU = 0, 4
QUAD_UP = (4, 28)
N_UP = FB // 2
QUAD_DOWN = (QUAD_UP[0] + N_UP, QUAD_UP[1] + N_UP)
N_DOWN = 4
QUAD_KV = QUAD_DOWN[0] + 2 * N_DOWN
QUAD_Q = QUAD_KV + 1
QUAD_WO = QUAD_Q + 2
assert QUAD_WO + 2 == QUAD_UP[1]

VEC = {"ln_ffn0": 0, "ln_mix1": 8, "ln_ffn1": 16, "ln_f": 24, "b_o": 32, "b_qkv": 40}
VECS = 52


def trunk(nc, x, meta_tokens, ln_mix, ln_ffn, lam_re, lam_im, log_dt, b_re, b_im, c_re, c_im,
          ssm_d, w_glu_a, w_glu_b, w_qkv, b_qkv, sinks, w_o, b_o, w_gate, w_up, w_down, ln_f, out):
    ctx = ExitStack()
    with ctx:
        def sb(name, shape, dt=F32, scope=ctx):
            return scope.enter_context(nc.sbuf_tensor(name, shape, dt))

        def sem(name):
            return ctx.enter_context(nc.semaphore(name))

        residual = sb("residual", [P, KB, L])
        raw = sb("raw", [P, 2, KB, 2 * P])
        w_high = sb("w_high", [P, 2, KB, P], F32R)
        skip = ExitStack()
        d_diag = sb("d_diag", [2 * GROUP, PAIRS, GROUP], scope=skip)
        skip.close()
        w_low = sb("w_low", [P, 2, KB, P], F32R)
        diag_mask = sb("diag_mask", [2 * GROUP, GROUP])
        ident = sb("ident", [P, P])
        ones = sb("ones", [P, P])
        neg_half = sb("neg_half", [P, 8])
        vecs_row = sb("vecs_row", [VECS, P])
        vecs = sb("vecs", [P, VECS])
        q_bias = sb("q_bias", [P, KB])
        sink_row = sb("sink_row", [P, HEADS])
        mean_sq = sb("mean_sq", [P, 8])
        rstd = sb("rstd", [P, 8])
        banks = ctx.enter_context(nc.psum_tensor("banks", [P, 8, 512], F32))
        y_dram = nc.dram_tensor("y_dram", (BATCHES, T, GROUP, GB, C), F32, kind="Internal").ap()
        k_dram = nc.dram_tensor("k_dram", (BATCHES, GROUP, 2, PB, 2 * T - 1, GROUP), F32, kind="Internal").ap()

        early = ExitStack()
        row = {k: sb("row_" + k, [PAIRS, P], scope=early) for k in ("lam_re", "lam_im", "decay_arg", "angle")}
        cols_in = sb("cols_in", [P, 4, PAIRS], scope=early)
        col = {k: sb("col_" + k, [P, PAIRS], scope=early) for k in (
            "turns", "abs_angle", "sin", "cos", "mag", "t0", "t1", "t2", "t3", "lr1")}
        two = sb("two", [P, PAIRS], scope=early)
        dt_log = sb("dt_log", [PAIRS, 2], scope=early)
        dt_log2 = sb("dt_log2", [PAIRS, 2], scope=early)
        dt_row = sb("dt_row", [PAIRS, 2], scope=early)
        gain_nat = sb("gain_nat", [P, PAIRS, GROUP], scope=early)
        gain_diag = sb("gain_diag", [2 * GROUP, PAIRS, GROUP], scope=early)
        table_t = sb("table_t", [P, 2, PAIRS, TA // 2], scope=early)
        early.close()
        gate = sb("gate", [P, 2, L])
        prod = sb("prod", [P, 2, L])
        square = sb("square", [P, L])
        sq_sum = sb("sq_sum", [P, L])
        rstd_row = sb("rstd_row", [P, L])
        diag = sb("diag", [P, L])

        tokens = ExitStack()
        xt = sb("xt", [C, T, D], scope=tokens)
        tokens.close()
        after_mixer = ExitStack()
        glu_high = sb("glu_high", [P, KB, L], F32R, scope=after_mixer)
        glu_low = sb("glu_low", [P, KB, L], F32R, scope=after_mixer)

        s5 = ExitStack()
        loaded = ExitStack()
        braw = {k: sb("raw_" + k, [PAIRS, 2 * STATE * GROUP], scope=loaded) for k in ("b_re", "b_im", "c_re", "c_im")}
        loaded.close()
        inj = sb("inj", [P, 2, PB, T, GROUP], scope=s5)
        inj_t = sb("inj_t", [P, PB, T, GROUP], scope=s5)
        inj_T = sb("inj_T", [P, PB, 2, P], scope=s5)
        read = sb("read", [P, 3, 2, PB, T + 1, GROUP], scope=s5)
        read_t = sb("read_t", [P, PB, T, GROUP], scope=s5)
        k_lag = sb("k_lag", [2 * GROUP, PB, T, GROUP], scope=s5)
        k_toep = sb("k_toep", [P, 2, GB, P], scope=s5)
        turn = sb("turn", [P, 2, 2, PB, CS], scope=s5)
        turn_t = sb("turn_t", [P, 2, PB, TA, TA], scope=s5)
        decay_row = sb("decay_row", [P, PB, CS], scope=s5)
        rows_only = ExitStack()
        u_row = sb("u_row", [C, 2, 16, T, GROUP], scope=rows_only)
        rows_only.close()
        z = sb("z", [P, 2, PB, CS], scope=s5)
        zt = sb("zt", [P, 2, PB, CS], scope=s5)
        zs = sb("zs", [P, 2, PB, CS], scope=s5)
        state = sb("state", [P, 2, PB, CS], scope=s5)
        y_act = sb("y_act", [P, 2, GB, C], scope=s5)
        y_feat = sb("y_feat", [P, 2, T, C], scope=s5)
        u_state = sb("u_state", [P, GROUPS, C], scope=s5)
        nat = {k: sb("nat_" + k, [P, PAIRS, GROUP], scope=s5) for k in ("b_re", "b_im", "c_re", "neg_c_im")}
        bbar_pair = sb("bbar_pair", [P, 2, PAIRS, 2 * GROUP], scope=s5)
        lam_t = sb("lam_t", [P, len(LAM_NAMES), PAIRS], scope=s5)
        powr = sb("powr", [P, 2, T + 1, PAIRS], scope=s5)
        fine = sb("fine", [P, 2, PAIRS, TA + 1], scope=s5)
        coarse = sb("coarse", [P, 2, PAIRS, TA + 1], scope=s5)
        pow_t = sb("pow_t", [P, 2, 4, PAIRS], scope=s5)
        s5.close()
        after_mixer.close()

        att = ExitStack()
        q_t = sb("q_t", [P, 2, 2, SEQ], scope=att)
        k_t = sb("k_t", [P, 2, 2, L], scope=att)
        v_t = sb("v_t", [P, 2, L], scope=att)
        v_meta_t = sb("v_meta_t", [P, 2, 4, 4 * META], scope=att)
        v_win = sb("v_win", [P, WINDOWS, KV_HEADS * HD], scope=att)
        v_meta = sb("v_meta", [4 * META, 4, KV_HEADS * HD], scope=att)
        prob_e = sb("prob_e", [P, 2, 2, WIN], scope=att)
        prob_b = sb("prob_b", [P, 2, 4, BAND], scope=att)
        prob_m = sb("prob_m", [P, 2, 4, META], scope=att)
        prob_tb = sb("prob_tb", [P, 2, 4, P], scope=att)
        prob_tm = sb("prob_tm", [4 * META, 2, P], scope=att)
        neg_sink = sb("neg_sink", [P, KV_HEADS, 2], scope=att)
        row_max = sb("row_max", [P, 2, 2], scope=att)
        neg_max = sb("neg_max", [P, 2, 2, 2], scope=att)
        sink_exp = sb("sink_exp", [P, 2, 2, 2], scope=att)
        denom = sb("denom", [P, 2, 2, 2], scope=att)
        o_high = sb("o_high", [P, KB, SEQ], F32R, scope=att)
        o_low = sb("o_low", [P, KB, SEQ], F32R, scope=att)
        att.close()

        fin = ExitStack()
        out_row = sb("out_row", [P, 4, D], scope=fin)
        fin.close()

        a_high = sb("a_high", [P, FB, L], F32R)
        a_low = sb("a_low", [P, FB, L], F32R)
        last_input = ExitStack()
        scaled = sb("scaled", [P, KB, L], scope=last_input)
        last_input.close()
        x_high = sb("x_high", [P, KB, L], F32R)
        x_low = sb("x_low", [P, KB, L], F32R)

        raw_loaded = [sem("raw_loaded0"), sem("raw_loaded1")]
        rows_loaded, bc_loaded, consts_loaded, gain_loaded = sem("rows_loaded"), sem("bc_loaded"), sem("consts_loaded"), sem("gain_loaded")
        x_loaded = [sem(f"x_loaded{i}") for i in range(4)]
        toep_placed, keys_swapped, out_stored = sem("toep_placed"), sem("keys_swapped"), sem("out_stored")
        w_rounded, w_split, w_used = sem("w_rounded"), sem("w_split"), sem("w_used")
        gate_ready, gate_scaled, pre_ready = sem("gate_ready"), sem("gate_scaled"), sem("pre_ready")
        up_taken, added, a_rounded, a_split = sem("up_taken"), sem("added"), sem("a_rounded"), sem("a_split")
        squared, sq_added = sem("squared"), sem("sq_added")
        mean_summed, mean_taken, rstd_ready = sem("mean_summed"), sem("mean_taken"), sem("rstd_ready")
        diag_ready, rstd_spread, rstd_copied = sem("diag_ready"), sem("rstd_spread"), sem("rstd_copied")
        x_rounded, x_split = sem("x_rounded"), sem("x_split")
        dve_step, pool_step = sem("dve_step"), sem("pool_step")
        consts_made, dt_ready, mag_ready, lam_ready = sem("consts_made"), sem("dt_ready"), sem("mag_ready"), sem("lam_ready")
        dt_arg, mag_arg, angle_ready, trig_ready, rows_ready = sem("dt_arg"), sem("mag_arg"), sem("angle_ready"), sem("trig_ready"), sem("rows_ready")
        vecs_t, vecs_ready, rows_t = sem("vecs_t"), sem("vecs_ready"), sem("rows_t")
        nat_tr, nat_copied, nat_ready = sem("nat_tr"), sem("nat_copied"), sem("nat_ready")
        x_squared, mean_ready0, rstd0 = sem("x_squared"), sem("mean_ready0"), sem("rstd0")
        res_t, res_copied, u_normed, u_tr, u_copied = sem("res_t"), sem("res_copied"), sem("u_normed"), sem("u_tr"), sem("u_copied")
        inj_ready, inj_tr, inj_copied = sem("inj_ready"), sem("inj_tr"), sem("inj_copied")
        turn_ready, read_ready = sem("turn_ready"), sem("read_ready")
        v_ready, v_taken, k_ready, k_copied, zeros_made = sem("v_ready"), sem("v_taken"), sem("k_ready"), sem("k_copied"), sem("zeros_made")
        skip_joined, state_ready, y_ready, gelu_ready, y_placed, y_stored, bbar_placed = sem("skip_joined"), sem("state_ready"), sem("y_ready"), sem("gelu_ready"), sem("y_placed"), sem("y_stored"), sem("bbar_placed")
        gt_rounded, gt_split, pairs_cleared = sem("gt_rounded"), sem("gt_split"), sem("pairs_cleared")
        fine_ready, powers_ready, k_stored, zeros_stored = sem("fine_ready"), sem("powers_ready"), sem("k_stored"), sem("zeros_stored")
        kv_scaled, kv_ready, v_meta_ready, v_tr, v_rows_ready = sem("kv_scaled"), sem("kv_ready"), sem("v_meta_ready"), sem("v_tr"), sem("v_rows_ready")
        q_scaled, q_ready, scores_ready, shifted, prob_ready = sem("q_scaled"), sem("q_ready"), sem("scores_ready"), sem("shifted"), sem("prob_ready")
        prob_scaled, prob_tr, prob_t_ready = sem("prob_scaled"), sem("prob_tr"), sem("prob_t_ready")
        o_ready, o_rounded, o_split = sem("o_ready"), sem("o_rounded"), sem("o_split")
        scaled_ready, out_tr, out_left, out_right = sem("scaled_ready"), sem("out_tr"), sem("out_left"), sem("out_right")

        block = ctx.enter_context(nc.Block())

        def halves(n):
            return [(0, HALF), (HALF, HALF)] if n == L else [(META, SEQ)]

        def bank_view(first, n):
            return banks[:, first:first + 2, 0:HALF] if n == L else banks[:, first, 0:SEQ]

        def cols(ap, n):
            return ap.rearrange("p (h c) -> p h c", h=2) if n == L else ap[:, META:L]

        def norm_tiles(n):
            return (88, 6, 0) if n == L else (128, 4, META)

        def rows(ap, m, a=0, e=L):
            return ap[:, m, a:e] if isinstance(m, int) else ap[:, bass.ds(m, 1), a:e].rearrange("p o c -> p (o c)")

        def gain_of(name, m):
            return vecs[:, VEC[name] + m:VEC[name] + m + 1] if isinstance(m, int) else vecs[:, bass.ds(m + VEC[name], 1)]

        def rstd_banks(n):
            return banks[:, 6:8, 0:HALF] if n == L else banks[:, 7, :]

        def scores_of(s):
            b0 = 2 + 2 * (s % 2)
            return banks[:, b0:b0 + 2, 0:2 * WIN].rearrange("p h (c k) -> p h c k", c=2)

        def meta_of(s):
            return banks[0:4 * META, 2 + 2 * (s % 2), 2 * WIN:2 * WIN + P]

        def heads_out(o, s):
            kv, b = s // BLOCKS, s % BLOCKS
            return o[:, 2 * kv:2 * kv + 2, b * QB:(b + 1) * QB].rearrange("p j (c q) -> p c j q", c=2)

        @block.sync
        def _(sp):
            def load_tile(quad, tile, src, rows=KB, wait=True):
                if wait:
                    sp.wait_ge(w_split, 4 * quad + 2 * tile - 2)
                sp.dma_start(raw[:, tile, 0:rows, :], src).then_inc(raw_loaded[tile], 16)

            def by_rows(w):
                return w.rearrange("(k p) n -> p k n", p=P)

            def place_lags(b):
                sp.wait_ge(skip_joined, b + 1)
                for j in range(2):
                    sp.dma_start(k_dram[b, :, j, :, T - 1:, :].rearrange("q r t c -> q r (t c)"),
                                 k_lag[j * GROUP:(j + 1) * GROUP].rearrange("q r t c -> q r (t c)")).then_inc(k_stored, 16)
                if b == 0:
                    sp.wait_ge(zeros_stored, 16)
                if b >= 2:
                    sp.wait_ge(y_ready, b - 1)
                sp.wait_ge(k_stored, 32 * (b + 1))
                for s in range(T):
                    sp.dma_start(
                        k_toep[(T - 1 - s) * GROUP:(T - s) * GROUP, b % 2],
                        k_dram[b, :, :, :, T - 1 - s:2 * T - 1 - s, :].rearrange("q j r t c -> q (j r) (t c)"),
                    ).then_inc(toep_placed, 16)

            sp.dma_start(row["lam_re"][:], lam_re.rearrange("o (r j) n -> (o r) (j n)", j=2)).then_inc(rows_loaded, 16)
            sp.dma_start(row["lam_im"][:], lam_im.rearrange("o (r j) n -> (o r) (j n)", j=2)).then_inc(rows_loaded, 16)
            sp.dma_start(dt_log[:], log_dt.rearrange("o (r j) -> (o r) j", j=2)).then_inc(rows_loaded, 16)
            xv = x.rearrange("o (c s) d -> (o c) s d", s=T)
            mv = meta_tokens.rearrange("(c s) d -> c s d", s=T)
            for i in range(4):
                sp.dma_start(xt[META // T:C, 2 * i:2 * i + 2, :], xv[:, 2 * i:2 * i + 2, :]).then_inc(x_loaded[i], 16)
                sp.dma_start(xt[0:META // T, 2 * i:2 * i + 2, :], mv[:, 2 * i:2 * i + 2, :]).then_inc(x_loaded[i], 16)
            for k, w in (("b_re", b_re), ("b_im", b_im)):
                sp.dma_start(braw[k][:], w.rearrange("o (r j) n q -> (o r) (j n q)", j=2)).then_inc(bc_loaded, 16)
            for k, w in (("c_re", c_re), ("c_im", c_im)):
                for j in range(2):
                    sp.dma_start(braw[k][:].rearrange("r (q j n) -> r q j n", q=GROUP, j=2)[:, :, j, :],
                                 w.rearrange("o (r j) q n -> (o r) j q n", j=2)[:, j]).then_inc(bc_loaded, 16)
            gain_v = ln_mix[0:1].rearrange("o (r j q) -> o j r q", j=2, q=GROUP)
            for j in range(2):
                sp.dma_start(gain_nat[j * STATE:(j + 1) * STATE], gain_v[:, j].to_broadcast([STATE, PAIRS, GROUP])).then_inc(gain_loaded, 16)
            for j in range(2):
                sp.dma_start(gain_diag[j * GROUP:(j + 1) * GROUP], gain_v[:, j].to_broadcast([GROUP, PAIRS, GROUP])).then_inc(consts_loaded, 16)
                sp.dma_start(d_diag[j * GROUP:(j + 1) * GROUP],
                             ssm_d.rearrange("o (r j q) -> o j r q", j=2, q=GROUP)[:, j].to_broadcast([GROUP, PAIRS, GROUP])).then_inc(consts_loaded, 16)
            sp.dma_start(sink_row[:], sinks[0:1, :].to_broadcast([P, HEADS])).then_inc(consts_loaded, 16)
            for name, v, n in (("ln_ffn0", ln_ffn[0], KB), ("ln_mix1", ln_mix[1], KB), ("ln_ffn1", ln_ffn[1], KB),
                               ("ln_f", ln_f, KB), ("b_o", b_o[0], KB), ("b_qkv", b_qkv[0], 12)):
                sp.dma_start(vecs_row[VEC[name]:VEC[name] + n, :], v.rearrange("(k p) -> k p", p=P)).then_inc(consts_loaded, 16)
            for i in range(N_GLU):
                if i == 1:
                    sp.wait_ge(zeros_made, 1)
                    sp.dma_start(k_dram.rearrange("b q j r t c -> (b q j r) (t c)")[:, 0:(T - 1) * GROUP].rearrange("(p m) n -> p m n", p=P),
                                 k_toep[:, 0, 0:BATCHES, 0:(T - 1) * GROUP]).then_inc(zeros_stored, 16)
                    place_lags(0)
                    for b in range(BATCHES):
                        if b + 1 < BATCHES:
                            place_lags(b + 1)
                load_tile(i, 0, by_rows(w_glu_b[0])[:, :, 2 * P * i:2 * P * (i + 1)], wait=i > 0)
                load_tile(i, 1, by_rows(w_glu_a[0])[:, :, 2 * P * i:2 * P * (i + 1)], wait=i > 0)

            def load_ffn(layer):
                with sp.Fori(0, N_UP, 1) as i:
                    load_tile(QUAD_UP[layer] + i, 0, by_rows(w_gate[layer])[:, :, bass.ds(i * (2 * P), 2 * P)])
                    load_tile(QUAD_UP[layer] + i, 1, by_rows(w_up[layer])[:, :, bass.ds(i * (2 * P), 2 * P)])
                with sp.Fori(0, N_DOWN, 1) as i:
                    for t, (k0, nk) in enumerate(DOWN_TILES):
                        load_tile(QUAD_DOWN[layer] + 2 * i + t // 2, t % 2,
                                  by_rows(w_down[layer])[:, k0:k0 + nk, bass.ds(i * (2 * P), 2 * P)], rows=nk)

            load_ffn(0)
            qkv = by_rows(w_qkv[0])
            load_tile(QUAD_KV, 0, qkv[:, :, HEADS * HD:HEADS * HD + 2 * P])
            load_tile(QUAD_KV, 1, qkv[:, :, HEADS * HD + 2 * P:HEADS * HD + 4 * P])
            for kv in range(2):
                load_tile(QUAD_Q, kv, qkv[:, :, 2 * P * kv:2 * P * (kv + 1)])
            sp.wait_ge(kv_ready, 2)
            sp.dma_start(k_t[0:HD, :, 1, :], k_t[HD:P, :, 0, :]).then_inc(keys_swapped, 16)
            sp.dma_start(k_t[HD:P, :, 1, :], k_t[0:HD, :, 0, :]).then_inc(keys_swapped, 16)
            for kv in range(2, KV_HEADS):
                load_tile(QUAD_Q + kv // 2, kv % 2, qkv[:, :, 2 * P * kv:2 * P * (kv + 1)])
            for i in range(4):
                load_tile(QUAD_WO + i // 2, i % 2, by_rows(w_o[0])[:, :, 2 * P * i:2 * P * (i + 1)])
            load_ffn(1)
            for j in range(4):
                sp.wait_ge(out_left, j + 1)
                sp.wait_ge(out_right, j + 1)
                sp.dma_start(out[0, j * P:(j + 1) * P, :], out_row[:, j, :]).then_inc(out_stored, 16)
            sp.wait_ge(out_stored, 64)

        @block.gpsimd
        def _(pool):
            steps = [0]

            def step(ins):
                ins.then_inc(pool_step, 1)
                steps[0] += 1
                pool.wait_ge(pool_step, steps[0])

            nc.gpsimd.memset(ones[:], 1.0)
            nc.gpsimd.memset(neg_half[:], -0.5)
            nc.gpsimd.memset(two[:], 2.0)
            nc.gpsimd.memset(bbar_pair[:], 0.0).then_inc(pairs_cleared, 1)
            step(nc.gpsimd.memset(ident[:], 0.0))
            nc.gpsimd.affine_select(out=ident[:], in_=ident[:], compare_op=ALU.not_equal, fill=1.0, base=0,
                                    pattern=[[-1, P]], channel_multiplier=1).then_inc(consts_made, 1)
            pool.wait_ge(dt_arg, 1)
            nc.gpsimd.tensor_tensor(dt_row[:], two[0:PAIRS, 0:2], dt_log2[:], ALU.pow).then_inc(dt_ready, 1)
            pool.wait_ge(mag_arg, 1)
            nc.gpsimd.tensor_tensor(col["mag"][:], two[:], cols_in[:, 2], ALU.pow).then_inc(mag_ready, 1)
            pool.wait_ge(mean_ready0, 1)
            nc.gpsimd.tensor_tensor(rstd[0:C, 0:T], mean_sq[0:C, 0:T], neg_half[0:C, 0:T], ALU.pow).then_inc(rstd0, 1)

            def cmul(dr, di, ar, ai, br, bi, t0, t1):
                nc.gpsimd.tensor_tensor(dr, ar, br, ALU.mult)
                nc.gpsimd.tensor_tensor(t0, ai, bi, ALU.mult)
                nc.gpsimd.tensor_tensor(di, ar, bi, ALU.mult)
                step(nc.gpsimd.tensor_tensor(t1, ai, br, ALU.mult))
                nc.gpsimd.tensor_tensor(dr, dr, t0, ALU.subtract)
                step(nc.gpsimd.tensor_tensor(di, di, t1, ALU.add))

            pool.wait_ge(fine_ready, 1)
            for tab, first in ((coarse, fine[:, :, :, TA]),):
                nc.gpsimd.memset(tab[:, 0, :, 0:1], 1.0)
                nc.gpsimd.memset(tab[:, 1, :, 0:1], 0.0)
                step(nc.gpsimd.tensor_copy(tab[:, :, :, 1], first))
                k = 1
                while k < TA:
                    shape = [P, PAIRS, k]
                    cmul(tab[:, 0, :, k + 1:2 * k + 1], tab[:, 1, :, k + 1:2 * k + 1], tab[:, 0, :, 1:k + 1], tab[:, 1, :, 1:k + 1],
                         tab[:, 0, :, k:k + 1].to_broadcast(shape), tab[:, 1, :, k:k + 1].to_broadcast(shape),
                         table_t[:, 0, :, 0:k], table_t[:, 1, :, 0:k])
                    k *= 2

            def turns(b):
                pr = slice(b * PB, (b + 1) * PB)
                if b >= 2:
                    pool.wait_ge(state_ready, b - 1)
                if b >= 1:
                    pool.wait_ge(turn_ready, b)
                shape = [P, PB, TA, TA]
                fr, fi = (fine[:, i, pr, 0:TA].unsqueeze(2).to_broadcast(shape) for i in range(2))
                gr, gi = (coarse[:, i, pr, 0:TA].unsqueeze(3).to_broadcast(shape) for i in range(2))
                tr, ti = (turn[:, b % 2, i, :, 0:TA * TA].rearrange("p r (a f) -> p r a f", f=TA) for i in range(2))
                nc.gpsimd.tensor_tensor(tr, gr, fr, ALU.mult)
                nc.gpsimd.tensor_tensor(turn_t[:, 0], gi, fi, ALU.mult)
                nc.gpsimd.tensor_tensor(ti, gr, fi, ALU.mult)
                step(nc.gpsimd.tensor_tensor(turn_t[:, 1], gi, fr, ALU.mult))
                nc.gpsimd.tensor_copy(turn[:, b % 2, 0, :, TA * TA], coarse[:, 0, pr, TA])
                nc.gpsimd.tensor_copy(turn[:, b % 2, 1, :, TA * TA], coarse[:, 1, pr, TA])
                nc.gpsimd.tensor_tensor(tr, tr, turn_t[:, 0], ALU.subtract)
                nc.gpsimd.tensor_tensor(ti, ti, turn_t[:, 1], ALU.add).then_inc(turn_ready, 1)

            def reads(b):
                pr = slice(b * PB, (b + 1) * PB)
                if b >= 3:
                    pool.wait_ge(y_ready, b - 2)
                rr, ri = read[:, b % 3, 0], read[:, b % 3, 1]
                cr = nat["c_re"][:, pr, :].unsqueeze(2)
                ci = nat["neg_c_im"][:, pr, :].unsqueeze(2)
                shape = [P, PB, T, GROUP]
                lr = powr[:, 0, 1:T + 1, pr].rearrange("p t r -> p r t").unsqueeze(3).to_broadcast(shape)
                li = powr[:, 1, 1:T + 1, pr].rearrange("p t r -> p r t").unsqueeze(3).to_broadcast(shape)
                crb, cib = cr.to_broadcast(shape), ci.to_broadcast(shape)
                nc.gpsimd.tensor_copy(rr[:, :, 0, :], nat["c_re"][:, pr, :])
                nc.gpsimd.tensor_copy(ri[:, :, 0, :], nat["neg_c_im"][:, pr, :])
                nc.gpsimd.tensor_tensor(rr[:, :, 1:, :], crb, lr, ALU.mult)
                step(nc.gpsimd.tensor_tensor(read_t[:], cib, li, ALU.mult))
                nc.gpsimd.tensor_tensor(rr[:, :, 1:, :], rr[:, :, 1:, :], read_t[:], ALU.add)
                step(nc.gpsimd.tensor_tensor(ri[:, :, 1:, :], cib, lr, ALU.mult))
                step(nc.gpsimd.tensor_tensor(read_t[:], crb, li, ALU.mult))
                nc.gpsimd.tensor_tensor(ri[:, :, 1:, :], ri[:, :, 1:, :], read_t[:], ALU.subtract).then_inc(read_ready, 1)

            pool.wait_ge(nat_copied, 4)
            nc.gpsimd.memset(k_toep[:, 0], 0.0).then_inc(zeros_made, 1)
            pool.wait_ge(powers_ready, 1)
            reads(0)
            pool.wait_ge(nat_ready, 1)
            turns(0)
            for b in range(1, BATCHES):
                turns(b)
                reads(b)

            def norm(index, n):
                tt, nt, _ = norm_tiles(n)
                pool.wait_ge(mean_taken, index + 1)
                nc.gpsimd.tensor_tensor(rstd[0:tt, 0:nt], mean_sq[0:tt, 0:nt], neg_half[0:tt, 0:nt],
                                        ALU.pow).then_inc(rstd_ready, 1)

            def feed_forward(layer, n, it0):
                a, e = (0, L) if n == L else (META, L)
                with pool.Fori(0, N_UP, 1) as i:
                    for j in range(2):
                        pool.wait_ge(gate_ready, 2 * i + (2 * it0 + j + 1))
                        nc.gpsimd.tensor_tensor(gate[:, j, a:e], gate[:, j, a:e], rstd_row[:, a:e], ALU.mult).then_inc(gate_scaled, 1)

            norm(0, L)
            feed_forward(0, L, N_GLU)
            norm(1, L)
            pool.wait_ge(w_used, 4 * QUAD_KV)
            step(nc.gpsimd.memset(v_meta_t[:], 0.0))
            pool.wait_ge(kv_ready, 4)
            for i in range(4):
                ins = nc.gpsimd.tensor_copy(v_meta_t[:, :, i, i * META:(i + 1) * META], v_t[:, :, 0:META])
            ins.then_inc(v_meta_ready, 1)
            norm(2, SEQ)
            feed_forward(1, SEQ, N_GLU + N_UP)
            norm(3, SEQ)

        @block.scalar
        def _(act):
            def round_weights(quad, off, wait=True):
                quad, off = quad + off // 4, off % 4
                slot, j = off // 2, off % 2
                act.wait_ge(raw_loaded[slot], 16 * (quad + 1))
                if wait:
                    act.wait_ge(w_used, 4 * quad + off - 1)
                nc.scalar.copy(w_high[:, j], raw[:, slot, :, j * P:(j + 1) * P]).then_inc(w_rounded, 1)

            act.wait_ge(angle_ready, 1)
            nc.scalar.activation(col["sin"][:], cols_in[:, 3], ACT.Sin)
            nc.scalar.activation(col["cos"][:], col["abs_angle"][:], ACT.Sin).then_inc(trig_ready, 1)
            for s in range(T):
                if s % 2 == 0:
                    act.wait_ge(x_loaded[s // 2], 32)
                if s > 0:
                    act.wait_ge(x_squared, s)
                nc.scalar.activation(banks[0:C, 6:8, :], xt[:, s, :].rearrange("c (h n) -> c h n", h=2), ACT.Square, accum_out=mean_sq[0:C, s:s + 1]).then_inc(x_squared, 1)
            act.wait_ge(rstd0, 1)
            for i in range(5):
                if i < 4:
                    if i >= 2:
                        act.wait_ge(u_tr, 2 * i - 2)
                    for s in range(T):
                        ins = nc.scalar.mul(u_row[:, i % 2, :, T - 1 - s, :], xt[:, s, i * 256:(i + 1) * 256].rearrange("c (g q) -> c g q", q=GROUP),
                                            rstd[0:C, s:s + 1])
                    ins.then_inc(u_normed, 1)
                for h in range(2 * i - 2, 2 * i):
                    if i >= 1:
                        act.wait_ge(u_tr, h + 1)
                        b0 = 2 * (h % 2)
                        nc.scalar.copy(u_state[:, 8 * h:8 * h + 8, :].rearrange("p (h g) c -> p h (g c)", h=2),
                                       banks[:, b0:b0 + 2, 0:4 * C]).then_inc(u_copied, 1)
            act.wait_ge(vecs_t, 1)
            nc.scalar.copy(vecs[:], banks[:, 4, 0:VECS]).then_inc(vecs_ready, 1)
            act.wait_ge(vecs_ready, 1)
            nc.scalar.mul(q_bias[:], vecs[:, VEC["b_qkv"]:VEC["b_qkv"] + KB], SCALE)

            def front(b):
                act.wait_ge(inj_tr, b + 1)
                if b >= 1:
                    act.wait_ge(v_ready, b)
                nc.scalar.copy(inj_T[:].rearrange("p r i n -> p (r i n)").rearrange("p (h n) -> p h n", h=2),
                               banks[:, 0:2, :]).then_inc(inj_copied, 1)

            def lags(b):
                act.wait_ge(k_ready, b + 1)
                if b >= 1:
                    act.wait_ge(k_stored, 32 * b)
                nc.scalar.copy(k_lag[:].rearrange("q r t c -> q (r t c)"), banks[0:2 * GROUP, 4 + b % 2, :]).then_inc(k_copied, 1)

            def gelu(b):
                act.wait_ge(y_ready, b + 1)
                if b >= 2:
                    act.wait_ge(y_stored, 16 * (b - 1))
                nc.scalar.activation(y_act[:, b % 2].rearrange("p (r j) c -> p j r c", j=2),
                                     banks[:, 6:8, 0:4 * C].rearrange("p j (r c) -> p j r c", r=PB),
                                     ACT.Gelu_apprx_tanh).then_inc(gelu_ready, 1)

            def store_outputs(b):
                act.wait_ge(gelu_ready, b + 1)
                nc.scalar.dma_start(y_dram[b].rearrange("s q g c -> (s q) (g c)"),
                                    y_act[:, b % 2].rearrange("p g c -> p (g c)")).then_inc(y_stored, 16)

            def load_outputs(b):
                act.wait_ge(y_stored, 16 * (b + 1))
                if b >= 2:
                    act.wait_ge(gt_split, b - 1)
                for g in range(GB):
                    nc.scalar.dma_start(y_feat[g * GROUP:(g + 1) * GROUP, b % 2],
                                        y_dram[b, :, :, g, :].rearrange("s q c -> q s c")).then_inc(y_placed, 16)

            def round_input(b):
                act.wait_ge(y_placed, 16 * GB * (b + 1))
                nc.scalar.copy(glu_high[:, b], y_feat[:, b % 2].rearrange("p s c -> p (s c)")).then_inc(gt_rounded, 1)

            front(0)
            lags(0)
            for b in range(BATCHES):
                if b + 1 < BATCHES:
                    front(b + 1)
                    if b >= 1:
                        load_outputs(b - 1)
                    lags(b + 1)
                else:
                    load_outputs(b - 1)
                if b >= 1:
                    round_input(b - 1)
                if b == BATCHES - 2:
                    round_weights(QUAD_GLU, 0, wait=False)
                    round_weights(QUAD_GLU, 1, wait=False)
                gelu(b)
                store_outputs(b)
            load_outputs(BATCHES - 1)
            round_input(BATCHES - 1)
            def updated(k, m, n, gain):
                act.wait_ge(added, k + 1)
                act.wait_ge(sq_added, k)
                a, e = (0, L) if n == L else (META, L)
                if gain != "ln_f":
                    nc.scalar.mul(rows(x_high, m, a, e), rows(residual, m, a, e), gain_of(gain, m)).then_inc(x_rounded, 1)
                nc.scalar.activation(square[:, a:e], rows(residual, m, a, e), ACT.Square).then_inc(squared, 1)

            def gated(quad, it, func, n):
                for j in range(2):
                    act.wait_ge(w_used, 4 * quad + j + 1)
                    if it > 0:
                        act.wait_ge(up_taken, 2 * it - 1 + j)
                    nc.scalar.activation(cols(gate[:, j], n), bank_view(2 * j, n), func).then_inc(gate_ready, 1)
                    round_weights(quad, 2 + j)
                for j in range(2):
                    round_weights(quad, 4 + j)

            for i in range(N_GLU):
                gated(QUAD_GLU + i, i, ACT.Sigmoid, L)
                for j in range(2):
                    updated(2 * i + j, 2 * i + j, L, "ln_ffn0")

            def spread_norm(index, n):
                act.wait_ge(rstd_spread, index + 1)
                nc.scalar.copy(cols(rstd_row[:], n), rstd_banks(n)).then_inc(rstd_copied, 1)

            def feed_forward(layer, n, it0, adds0, index, gain):
                a, e = (0, L) if n == L else (META, L)

                def up(i, first=False):
                    quad = QUAD_UP[layer] + i
                    for j in range(2):
                        round_weights(quad, 2 + j)
                        if first and j == 0:
                            spread_norm(index, n)
                        act.wait_ge(pre_ready, 2 * i + (2 * N_UP * layer + j + 1))
                        nc.scalar.activation(gate[:, j, a:e], gate[:, j, a:e], ACT.Silu).then_inc(gate_ready, 1)
                    for j in range(2):
                        round_weights(quad, 4 + j)
                        act.wait_ge(up_taken, 2 * i + (2 * it0 + j + 1))
                        nc.scalar.copy(rows(a_high, 2 * i + j, a, e), prod[:, j, a:e]).then_inc(a_rounded, 1)

                def down(i, last):
                    quad = QUAD_DOWN[layer] + 2 * i
                    for off in range(6):
                        round_weights(quad, 2 + off)
                    for j in range(2):
                        if not last:
                            round_weights(quad, 8 + j)
                        updated(2 * i + (adds0 + j), 2 * i + j, n, gain)

                up(0, first=True)
                with act.Fori(1, N_UP, 1) as i:
                    up(i)
                if layer == 0:
                    with act.Fori(0, N_DOWN, 1) as i:
                        down(i, False)
                else:
                    with act.Fori(0, N_DOWN - 1, 1) as i:
                        down(i, False)
                    down(N_DOWN - 1, True)

            feed_forward(0, L, N_GLU, KB, 0, "ln_mix1")
            for off in range(4):
                round_weights(QUAD_KV, 2 + off)
                if off == 0:
                    spread_norm(1, L)
                act.wait_ge(kv_scaled, off + 1)
                dst = k_t[:, off, 0, :] if off < 2 else v_t[:, off - 2, :]
                first = VEC["b_qkv"] + HEADS * HD // P + off
                nc.scalar.activation(dst, (gate if off < 2 else prod)[:, off % 2, :], ACT.Identity,
                                     bias=vecs[:, first:first + 1]).then_inc(kv_ready, 1)

            def query_block(i):
                kv, j = i // 2, i % 2
                act.wait_ge(q_scaled, i + 1)
                if kv >= 2:
                    act.wait_ge(scores_ready, (kv - 1) * BLOCKS)
                nc.scalar.activation(q_t[:, kv % 2, j, :], gate[:, j, 0:SEQ], ACT.Identity, scale=SCALE,
                                     bias=q_bias[:, i:i + 1]).then_inc(q_ready, 1)

            def exponentials(s):
                b = s % BLOCKS
                act.wait_ge(shifted, s + 1)
                for h, c in HALVES:
                    w = META + CHUNK if b == 0 and c == 0 else WIN
                    nc.scalar.activation(prob_e[:, h, c, 0:w], scores_of(s)[:, h, c, 0:w], ACT.Exp,
                                         bias=neg_max[:, s % 2, h, c:c + 1], accum_out=denom[:, s % 2, h, c:c + 1])
                nc.scalar.activation(sink_exp[:, s % 2], sink_exp[:, s % 2], ACT.Exp).then_inc(prob_ready, 1)

            def prob_transposed(s):
                act.wait_ge(prob_tr, s + 1)
                if s >= 2:
                    act.wait_ge(o_ready, s - 1)
                nc.scalar.copy(prob_tb[:, s % 2].rearrange("p i q -> p (i q)"), banks[:, 6, :])
                nc.scalar.copy(prob_tm[:, s % 2], meta_of(s)).then_inc(prob_t_ready, 1)

            def out_high(s):
                act.wait_ge(o_ready, s + 1)
                nc.scalar.copy(heads_out(o_high, s), banks[:, 7, 0:2 * P].rearrange("p (c j q) -> p c j q", c=2, j=2)).then_inc(o_rounded, 1)

            for i in range(2):
                round_weights(QUAD_Q, 2 + i)
                query_block(i)
            act.wait_ge(v_tr, 1)
            nc.scalar.copy(v_win[:].rearrange("p w n -> p (w n)")[:, 0:4 * 256].rearrange("p (b n) -> p b n", b=2), banks[:, 4:6, :])
            nc.scalar.copy(v_win[:, 4:6, :].rearrange("p w n -> p (w n)"), banks[:, 6, :])
            nc.scalar.copy(v_win[:, 6, :], banks[:, 7, 0:256])
            nc.scalar.copy(v_meta[:].rearrange("p i n -> p (i n)").rearrange("p (b n) -> p b n", b=2),
                           banks[0:4 * META, 2:4, :]).then_inc(v_rows_ready, 1)
            round_weights(QUAD_Q, 4)
            query_block(2)
            for s in range(STEPS + 2):
                if 1 <= s < STEPS + 1:
                    prob_transposed(s - 1)
                if s < STEPS:
                    exponentials(s)
                if s >= 2:
                    out_high(s - 2)
                if s % 2 and s < QUERY_STEPS:
                    i = FIRST_QUERIES + s // 2
                    round_weights(QUAD_Q, 2 + i)
                    query_block(i)
            for m in range(KB):
                round_weights(QUAD_WO, 2 + m)
                updated(2 * KB + m, m, SEQ, "ln_ffn1")
            feed_forward(1, SEQ, N_GLU + N_UP, 3 * KB, 2, "ln_f")
            act.wait_ge(rstd_ready, 4)
            for j in range(4):
                act.wait_ge(out_tr, j + 1)
                nc.scalar.mul(out_row[:, j, 0:D // 2], banks[:, 4 + j, :], rstd[:, j:j + 1]).then_inc(out_left, 1)

        @block.vector
        def _(dve):
            steps = [0]

            def mark(ins):
                ins.then_inc(dve_step, 1)
                steps[0] += 1

            def step(ins):
                mark(ins)
                dve.wait_ge(dve_step, steps[0])

            def split_weights(quad, off):
                quad, off = quad + off // 4, off % 4
                slot, j = off // 2, off % 2
                dve.wait_ge(w_rounded, 4 * quad + (off + 1))
                nc.vector.tensor_tensor(w_low[:, j], raw[:, slot, :, j * P:(j + 1) * P], w_high[:, j],
                                        ALU.subtract).then_inc(w_split, 1)

            TT, TS, STT = nc.vector.tensor_tensor, nc.vector.tensor_scalar, nc.vector.scalar_tensor_tensor
            r = {k: v[:] for k, v in row.items()}
            res_v = residual[:].rearrange("p k (c s) -> p k c s", s=T)
            dve.wait_ge(rows_loaded, 48)
            TS(dt_log2[:], dt_log[:], LOG2E, None, ALU.mult).then_inc(dt_arg, 1)
            step(TS(r["lam_re"], r["lam_re"], -1e-4, None, ALU.min))
            dve.wait_ge(dt_ready, 1)
            for j in range(2):
                h = slice(j * STATE, (j + 1) * STATE)
                TS(r["decay_arg"][:, h], r["lam_re"][:, h], dt_row[:, j:j + 1], LOG2E, ALU.mult, ALU.mult)
                ins = TS(r["angle"][:, h], r["lam_im"][:, h], dt_row[:, j:j + 1], None, ALU.mult)
            ins.then_inc(rows_ready, 1)
            dve.wait_ge(rows_t, 1)
            step(nc.vector.tensor_copy(cols_in[:], banks[:, 5, 0:4 * PAIRS].rearrange("p (k r) -> p k r", r=PAIRS)))
            r = {k: v[:] for k, v in col.items()}
            for i, k in enumerate(("lam_re", "lam_im", "decay_arg", "angle")):
                r[k] = cols_in[:, i]
            for i, k in enumerate(LAM_NAMES):
                r[k] = lam_t[:, i]
            TS(r["turns"], r["angle"], 1.0 / (2 * math.pi), ROUND, ALU.mult, ALU.add).then_inc(mag_arg, 1)
            dve.wait_ge(mag_arg, 1)
            step(TS(r["turns"], r["turns"], ROUND, None, ALU.subtract))
            step(STT(r["angle"], r["turns"], -TWO_PI_HIGH, r["angle"], ALU.mult, ALU.add))
            step(STT(r["angle"], r["turns"], -TWO_PI_LOW, r["angle"], ALU.mult, ALU.add))
            step(TS(r["angle"], r["angle"], PI_BELOW, -PI_BELOW, ALU.min, ALU.max))
            step(TS(r["abs_angle"], r["angle"], -1.0, None, ALU.mult))
            step(TT(r["abs_angle"], r["angle"], r["abs_angle"], ALU.max))
            TS(r["abs_angle"], r["abs_angle"], -1.0, math.pi / 2, ALU.mult, ALU.add).then_inc(angle_ready, 1)
            TT(r["t0"], r["lam_re"], r["lam_re"], ALU.mult)
            step(TT(r["t1"], r["lam_im"], r["lam_im"], ALU.mult))
            step(TT(r["t0"], r["t0"], r["t1"], ALU.add))
            nc.vector.reciprocal(r["t3"], r["t0"])
            for s in range(T):
                dve.wait_ge(res_t, s + 1)
                b0 = 2 * (s % 2)
                nc.vector.tensor_copy(res_v[:, :, :, s].rearrange("p (h k) c -> p h k c", h=2),
                                      banks[:, b0:b0 + 2, 0:4 * C].rearrange("p h (k c) -> p h k c", k=4)).then_inc(res_copied, 1)
            dve.wait_ge(x_squared, T)
            TS(mean_sq[0:C, 0:T], mean_sq[0:C, 0:T], 1.0 / D, EPS, ALU.mult, ALU.add).then_inc(mean_ready0, 1)

            def natural(i, k, sign):
                dve.wait_ge(nat_tr, i + 1)
                TS(nat[k][:].rearrange("p r q -> p q r"),
                   banks[:, 4 + i % 2, 0:GROUP * PAIRS].rearrange("p (q r) -> p q r", q=GROUP), sign, None, ALU.mult).then_inc(nat_copied, 1)

            natural(0, "b_re", 1.0)
            natural(1, "b_im", 1.0)
            dve.wait_ge(trig_ready, 1)
            dve.wait_ge(mag_ready, 1)
            TT(r["lam_bar_re"], r["mag"], r["cos"], ALU.mult)
            step(TT(r["lam_bar_im"], r["mag"], r["sin"], ALU.mult))
            step(TS(r["lr1"], r["lam_bar_re"], 1.0, None, ALU.subtract))
            TT(r["t0"], r["lr1"], r["lam_re"], ALU.mult)
            step(TT(r["t1"], r["lam_bar_im"], r["lam_im"], ALU.mult))
            step(TT(r["t0"], r["t0"], r["t1"], ALU.add))
            TT(r["w_re"], r["t0"], r["t3"], ALU.mult)
            TT(r["t2"], r["lam_bar_im"], r["lam_re"], ALU.mult)
            step(TT(r["t1"], r["lr1"], r["lam_im"], ALU.mult))
            step(TT(r["t2"], r["t2"], r["t1"], ALU.subtract))
            TT(r["w_im"], r["t2"], r["t3"], ALU.mult)
            TT(r["decay"], r["mag"], r["mag"], ALU.mult)
            step(TT(r["turn_re"], r["cos"], r["cos"], ALU.mult))
            step(TT(r["t1"], r["sin"], r["sin"], ALU.mult))
            TT(r["turn_im"], r["cos"], r["sin"], ALU.mult)
            step(TT(r["turn_re"], r["turn_re"], r["t1"], ALU.subtract))
            step(TS(r["turn_im"], r["turn_im"], 2.0, None, ALU.mult))
            for i in range(2):
                TT(r["t0"], r["turn_re"], r["turn_re"], ALU.mult)
                TT(r["t1"], r["turn_im"], r["turn_im"], ALU.mult)
                step(TT(r["t2"], r["turn_re"], r["turn_im"], ALU.mult))
                step(TT(r["decay"], r["decay"], r["decay"], ALU.mult))
                TT(r["turn_re"], r["t0"], r["t1"], ALU.subtract)
                ins = TS(r["turn_im"], r["t2"], 2.0, None, ALU.mult)
                if i == 0:
                    step(ins)
                else:
                    ins.then_inc(lam_ready, 1)
            dve.wait_ge(lam_ready, 1)

            def cmul(dr, di, ar, ai, br, bi, t0, t1):
                TT(dr, ar, br, ALU.mult)
                TT(t0, ai, bi, ALU.mult)
                TT(di, ar, bi, ALU.mult)
                step(TT(t1, ai, br, ALU.mult))
                TT(dr, dr, t0, ALU.subtract)
                step(TT(di, di, t1, ALU.add))

            pow_v = pow_t[:].rearrange("p i k r -> p i (k r)").rearrange("p i (r k) -> p i r k", k=4)
            nc.vector.memset(fine[:, 0, :, 0:1], 1.0)
            nc.vector.memset(fine[:, 1, :, 0:1], 0.0)
            step(nc.vector.tensor_copy(fine[:, :, :, 1], lam_t[:, 5:7, :]))
            k = 1
            while k < TA:
                s = [P, PAIRS, k]
                cmul(fine[:, 0, :, k + 1:2 * k + 1], fine[:, 1, :, k + 1:2 * k + 1], fine[:, 0, :, 1:k + 1], fine[:, 1, :, 1:k + 1],
                     fine[:, 0, :, k:k + 1].to_broadcast(s), fine[:, 1, :, k:k + 1].to_broadcast(s),
                     pow_v[:, 0, :, 0:k], pow_v[:, 1, :, 0:k])
                k *= 2
            natural(2, "c_re", 1.0)
            natural(3, "neg_c_im", -1.0)
            nc.vector.memset(pow_t[:, 0, 0, 0:1], 0.0).then_inc(fine_ready, 1)
            nc.vector.memset(powr[:, 0, 0], 1.0)
            nc.vector.memset(powr[:, 1, 0], 0.0)
            step(nc.vector.tensor_copy(powr[:, :, 1], lam_t[:, 0:2]))
            k = 1
            while k < T:
                s = [P, k, PAIRS]
                cmul(powr[:, 0, k + 1:2 * k + 1], powr[:, 1, k + 1:2 * k + 1], powr[:, 0, 1:k + 1], powr[:, 1, 1:k + 1],
                     powr[:, 0, k:k + 1].to_broadcast(s), powr[:, 1, k:k + 1].to_broadcast(s), pow_t[:, 0, 0:k], pow_t[:, 1, 0:k])
                k *= 2
            nc.vector.memset(pow_t[:, 0, 0, 0:1], 0.0).then_inc(powers_ready, 1)
            dve.wait_ge(nat_copied, 4)
            dve.wait_ge(gain_loaded, 32)
            TT(nat["b_re"][:], nat["b_re"][:], gain_nat[:], ALU.mult)
            step(TT(nat["b_im"][:], nat["b_im"][:], gain_nat[:], ALU.mult))
            wr = lam_t[:, 2].unsqueeze(2).to_broadcast([P, PAIRS, GROUP])
            wi = lam_t[:, 3].unsqueeze(2).to_broadcast([P, PAIRS, GROUP])
            nat_t = turn_t[:].rearrange("p i r a f -> p (i r a f)").rearrange("p (r q) -> p r q", q=GROUP)
            step(TT(nat_t, nat["b_re"][:], wi, ALU.mult))
            TT(nat["b_re"][:], nat["b_re"][:], wr, ALU.mult)
            sc = inj_t[:].rearrange("p r s q -> p (r s q)").rearrange("p (r q) -> p r q", q=GROUP)
            step(TT(sc, nat["b_im"][:], wi, ALU.mult))
            step(TT(nat["b_re"][:], nat["b_re"][:], sc, ALU.subtract))
            step(TT(nat["b_im"][:], nat["b_im"][:], wr, ALU.mult))
            TT(nat["b_im"][:], nat["b_im"][:], nat_t, ALU.add).then_inc(nat_ready, 1)
            dve.wait_ge(nat_ready, 1)
            dve.wait_ge(pairs_cleared, 1)
            for j in range(2):
                for i, part in enumerate(("b_re", "b_im")):
                    ins = nc.vector.tensor_copy(bbar_pair[j * STATE:(j + 1) * STATE, i, :, j * GROUP:(j + 1) * GROUP],
                                                nat[part][j * STATE:(j + 1) * STATE])
            ins.then_inc(bbar_placed, 1)

            def make_injection(b):
                pr = slice(b * PB, (b + 1) * PB)
                shape = [P, PB, T, GROUP]
                lr = powr[:, 0, 0:T, pr].rearrange("p t r -> p r t").unsqueeze(3).to_broadcast(shape)
                li = powr[:, 1, 0:T, pr].rearrange("p t r -> p r t").unsqueeze(3).to_broadcast(shape)
                br = nat["b_re"][:, pr, :].unsqueeze(2).to_broadcast(shape)
                bi = nat["b_im"][:, pr, :].unsqueeze(2).to_broadcast(shape)
                if b >= 1:
                    dve.wait_ge(inj_tr, b)
                TT(inj[:, 0], br, lr, ALU.mult)
                step(TT(inj_t[:], bi, li, ALU.mult))
                TT(inj[:, 0], inj[:, 0], inj_t[:], ALU.subtract)
                step(TT(inj[:, 1], bi, lr, ALU.mult))
                step(TT(inj_t[:], br, li, ALU.mult))
                TT(inj[:, 1], inj[:, 1], inj_t[:], ALU.add).then_inc(inj_ready, 1)

            make_injection(0)
            dve.wait_ge(consts_loaded, 11 * 16)
            dve.wait_ge(consts_made, 1)
            step(TT(diag_mask[:], ident[0:2 * GROUP, 0:GROUP], ident[0:2 * GROUP, GROUP:2 * GROUP], ALU.add))
            step(TT(d_diag[:], d_diag[:], gain_diag[:], ALU.mult))
            step(TT(d_diag[:], d_diag[:], diag_mask[:].unsqueeze(1).to_broadcast([2 * GROUP, PAIRS, GROUP]), ALU.mult))
            nc.vector.memset(decay_row[:], 0.0)
            flat = lambda ap: ap.rearrange("p r c -> p (r c)")
            def skip_joins(b):
                dve.wait_ge(k_copied, b + 1)
                TT(k_lag[:, :, 0, :], k_lag[:, :, 0, :], d_diag[:, b * PB:(b + 1) * PB, :], ALU.add).then_inc(skip_joined, 1)

            def split_input(b):
                dve.wait_ge(gt_rounded, b + 1)
                TT(glu_low[:, b], y_feat[:, b % 2].rearrange("p s c -> p (s c)"), glu_high[:, b], ALU.subtract).then_inc(gt_split, 1)

            skip_joins(0)
            make_injection(1)
            for b in range(BATCHES):
                pr = slice(b * PB, (b + 1) * PB)
                step(nc.vector.tensor_copy(decay_row[:, :, 1:], lam_t[:, 4, pr].unsqueeze(2).to_broadcast([P, PB, CS - 1])))
                tr, ti = turn[:, b % 2, 0], turn[:, b % 2, 1]
                vr = banks[:, 2, 0:PB * CS].rearrange("p (r c) -> p r c", r=PB)
                vi = banks[:, 3, 0:PB * CS].rearrange("p (r c) -> p r c", r=PB)
                dve.wait_ge(turn_ready, b + 1)
                dve.wait_ge(v_ready, b + 1)
                TT(z[:, 0], vr, tr, ALU.mult)
                TT(zt[:, 0], vi, ti, ALU.mult)
                TT(z[:, 1], vi, tr, ALU.mult)
                TT(zt[:, 1], vr, ti, ALU.mult).then_inc(v_taken, 1)
                dve.wait_ge(v_taken, b + 1)
                TT(z[:, 0], z[:, 0], zt[:, 0], ALU.add)
                step(TT(z[:, 1], z[:, 1], zt[:, 1], ALU.subtract))
                for i in range(2):
                    ins = nc.vector.tensor_tensor_scan(flat(zs[:, i]), flat(decay_row[:]), flat(z[:, i]), 0.0, ALU.mult, ALU.add)
                step(ins)
                TT(zt[:, 0], zs[:, 0], tr, ALU.mult)
                TT(zt[:, 1], zs[:, 1], ti, ALU.mult)
                TT(z[:, 0], zs[:, 0], ti, ALU.mult)
                step(TT(z[:, 1], zs[:, 1], tr, ALU.mult))
                if b >= 1:
                    dve.wait_ge(y_ready, b)
                TT(state[:, 0], zt[:, 0], zt[:, 1], ALU.subtract)
                TT(state[:, 1], z[:, 0], z[:, 1], ALU.add).then_inc(state_ready, 1)

                if b + 2 < BATCHES:
                    make_injection(b + 2)
                if b + 1 < BATCHES:
                    skip_joins(b + 1)
                if b >= 2:
                    split_input(b - 2)
                if b == BATCHES - 2:
                    dve.wait_ge(skip_joined, BATCHES)
                    split_weights(QUAD_GLU, 0)
                    split_weights(QUAD_GLU, 1)
            split_input(BATCHES - 2)
            split_input(BATCHES - 1)
            step(nc.vector.memset(sq_sum[:], 0.0))

            def updated(k, m, n, gain):
                a, e = (0, L) if n == L else (META, L)
                if gain != "ln_f":
                    dve.wait_ge(x_rounded, k + 1)
                    STT(rows(x_low, m, a, e), rows(residual, m, a, e), gain_of(gain, m), rows(x_high, m, a, e),
                        ALU.mult, ALU.subtract).then_inc(x_split, 1)
                else:
                    dve.wait_ge(added, k + 1)
                    TS(rows(scaled, m, a, e), rows(residual, m, a, e), gain_of(gain, m), None, ALU.mult).then_inc(scaled_ready, 1)
                dve.wait_ge(squared, k + 1)
                TT(sq_sum[:, a:e], sq_sum[:, a:e], square[:, a:e], ALU.add).then_inc(sq_added, 1)

            for i in range(N_GLU):
                quad = QUAD_GLU + i
                for j in range(2):
                    split_weights(quad, 2 + j)
                for j in range(2):
                    dve.wait_ge(w_used, 4 * quad + 2 + j + 1)
                    dve.wait_ge(gate_ready, 2 * i + j + 1)
                    TT(cols(prod[:, j], L), bank_view(4 + 2 * j, L), cols(gate[:, j], L), ALU.mult).then_inc(up_taken, 1)
                    dve.wait_ge(up_taken, 2 * i + j + 1)
                    res = residual[:, 2 * i + j].rearrange("p (c s) -> p s c", s=T)
                    TT(res, res, prod[:, j].rearrange("p (s c) -> p s c", s=T), ALU.add).then_inc(added, 1)
                    split_weights(quad, 4 + j)
                for j in range(2):
                    updated(2 * i + j, 2 * i + j, L, "ln_ffn0")

            def norm(index, n):
                tt, nt, _ = norm_tiles(n)
                dve.wait_ge(mean_summed, index + 1)
                TS(mean_sq[0:tt, 0:nt], banks[0:tt, 3 if index == 3 else 7, 0:nt], 1.0 / D, EPS, ALU.mult, ALU.add).then_inc(mean_taken, 1)
                if index == 3:
                    return
                nc.vector.memset(sq_sum[:], 0.0)
                dve.wait_ge(rstd_ready, index + 1)
                for t in range(nt):
                    ins = TS(diag[0:tt, t * tt:(t + 1) * tt], ident[0:tt, 0:tt], rstd[0:tt, t:t + 1], None, ALU.mult)
                ins.then_inc(diag_ready, 1)

            def feed_forward(layer, n, it0, adds0, index, gain):
                a, e = (0, L) if n == L else (META, L)

                def up(i, first=False):
                    quad = QUAD_UP[layer] + i
                    for j in range(2):
                        if first and j == 0:
                            split_weights(quad, 2)
                            dve.wait_ge(rstd_copied, index + 1)
                        dve.wait_ge(w_used, 4 * quad + (j + 1))
                        TT(cols(gate[:, j], n), bank_view(2 * j, n), cols(rstd_row[:], n), ALU.mult).then_inc(pre_ready, 1)
                        if not (first and j == 0):
                            split_weights(quad, 2 + j)
                    for j in range(2):
                        dve.wait_ge(w_used, 4 * quad + (2 + j + 1))
                        dve.wait_ge(gate_scaled, 2 * i + (2 * N_UP * layer + j + 1))
                        TT(cols(prod[:, j], n), bank_view(4 + 2 * j, n), cols(gate[:, j], n), ALU.mult).then_inc(up_taken, 1)
                        split_weights(quad, 4 + j)
                        dve.wait_ge(a_rounded, 2 * i + (2 * N_UP * layer + j + 1))
                        TT(rows(a_low, 2 * i + j, a, e), prod[:, j, a:e], rows(a_high, 2 * i + j, a, e),
                           ALU.subtract).then_inc(a_split, 1)

                def down(i, last):
                    quad = QUAD_DOWN[layer] + 2 * i
                    for off in range(6):
                        split_weights(quad, 2 + off)
                    for j in range(2):
                        dve.wait_ge(w_used, 4 * quad + (6 + j + 1))
                        r_m = rows(residual, 2 * i + j)
                        TT(cols(r_m, n), cols(r_m, n), bank_view(2 * j, n), ALU.add).then_inc(added, 1)
                        if not last:
                            split_weights(quad, 8 + j)
                        updated(2 * i + (adds0 + j), 2 * i + j, n, gain)

                up(0, first=True)
                with dve.Fori(1, N_UP, 1) as i:
                    up(i)
                if layer == 0:
                    with dve.Fori(0, N_DOWN, 1) as i:
                        down(i, False)
                else:
                    with dve.Fori(0, N_DOWN - 1, 1) as i:
                        down(i, False)
                    down(N_DOWN - 1, True)

            norm(0, L)
            feed_forward(0, L, N_GLU, KB, 0, "ln_mix1")
            norm(1, L)
            for j in range(2):
                TS(neg_sink[j * HD:(j + 1) * HD], sink_row[j * HD:(j + 1) * HD].rearrange("p (k j h) -> p k j h", k=KV_HEADS, j=2)[:, :, j, :],
                   -1.0, None, ALU.mult)
            for off in range(4):
                split_weights(QUAD_KV, 2 + off)
                if off == 0:
                    dve.wait_ge(rstd_copied, 2)
                dve.wait_ge(w_used, 4 * QUAD_KV + off + 1)
                TT(cols((gate if off < 2 else prod)[:, off % 2], L), bank_view(2 * off, L), cols(rstd_row[:], L), ALU.mult).then_inc(kv_scaled, 1)

            def query_block(i):
                dve.wait_ge(w_used, 4 * QUAD_Q + i + 1)
                if i < 2:
                    dve.wait_ge(kv_ready, 2)
                else:
                    dve.wait_ge(q_ready, i - 1)
                TT(gate[:, i % 2, 0:SEQ], banks[:, i % 2, :], rstd_row[:, META:], ALU.mult).then_inc(q_scaled, 1)

            def softmax_shift(s):
                kv, b = s // BLOCKS, s % BLOCKS
                dve.wait_ge(scores_ready, s + 1)
                sc = scores_of(s)
                if b == 0:
                    nc.vector.reduce_max(row_max[:, :, 0], sc[:, :, 0, 0:META + CHUNK], AX_X)
                    step(nc.vector.reduce_max(row_max[:, :, 1], sc[:, :, 1, :], AX_X))
                else:
                    step(nc.vector.reduce_max(row_max[:], sc, AX_X))
                ns = neg_sink[:, kv].unsqueeze(2).to_broadcast([P, 2, 2])
                step(STT(neg_max[:, s % 2], row_max[:], -1.0, ns, ALU.mult, ALU.min))
                TT(sink_exp[:, s % 2], neg_max[:, s % 2], ns, ALU.subtract).then_inc(shifted, 1)

            def normalize(s):
                b, i = s % BLOCKS, s % 2
                dve.wait_ge(prob_ready, s + 1)
                step(TT(denom[:, i], denom[:, i], sink_exp[:, i], ALU.add))
                step(nc.vector.reciprocal(denom[:, i], denom[:, i]))
                if s >= 2:
                    dve.wait_ge(prob_tr, s - 1)
                pb = prob_b[:, i].rearrange("p (h c) k -> p h c k", h=2)
                if b == 0:
                    for c, w in ((0, CHUNK), (1, BAND)):
                        TT(pb[:, :, c, 0:w], prob_e[:, :, c, META:META + w], denom[:, i, :, c:c + 1].to_broadcast([P, 2, w]), ALU.mult)
                else:
                    TT(pb, prob_e[:, :, :, META:], denom[:, i].unsqueeze(3).to_broadcast([P, 2, 2, BAND]), ALU.mult)
                TT(prob_m[:, i].rearrange("p (h c) k -> p h c k", h=2), prob_e[:, :, :, 0:META],
                   denom[:, i].unsqueeze(3).to_broadcast([P, 2, 2, META]), ALU.mult).then_inc(prob_scaled, 1)

            def out_low(s):
                dve.wait_ge(o_rounded, s + 1)
                TT(heads_out(o_low, s), banks[:, 7, 0:2 * P].rearrange("p (c j q) -> p c j q", c=2, j=2),
                   heads_out(o_high, s), ALU.subtract).then_inc(o_split, 1)

            for i in range(FIRST_QUERIES):
                split_weights(QUAD_Q, 2 + i)
                query_block(i)
            for s in range(STEPS + 2):
                if s < STEPS:
                    softmax_shift(s)
                    normalize(s)
                if s >= 2:
                    out_low(s - 2)
                if s % 2 and s < QUERY_STEPS:
                    i = FIRST_QUERIES + s // 2
                    query_block(i)
                    split_weights(QUAD_Q, 2 + i)
            for m in range(KB):
                dve.wait_ge(w_used, 4 * QUAD_WO + m + 1)
                STT(residual[:, m, META:], banks[:, m % 4, 0:SEQ], vecs[:, VEC["b_o"] + m:VEC["b_o"] + m + 1],
                    residual[:, m, META:], ALU.add, ALU.add).then_inc(added, 1)
                split_weights(QUAD_WO, 2 + m)
                updated(2 * KB + m, m, SEQ, "ln_ffn1")
            norm(2, SEQ)
            feed_forward(1, SEQ, N_GLU + N_UP, 3 * KB, 2, "ln_f")
            norm(3, SEQ)
            dve.wait_ge(rstd_ready, 4)
            for j in range(4):
                dve.wait_ge(out_tr, 4 + j + 1)
                TS(out_row[:, j, D // 2:], banks[:, j, :], rstd[:, j:j + 1], None, ALU.mult).then_inc(out_right, 1)

        @block.tensor
        def _(pe):
            def product(quad, off, first_k, nk, xh, xl, bank, n, start=True, stop=True, each=None, w_k=0, used=True):
                quad, off = quad + off // 4, off % 4
                j = off % 2
                pe.wait_ge(w_split, 4 * quad + (off + 1))
                parts = halves(n)
                for k in range(w_k, w_k + nk):
                    if each:
                        each(k)
                    for w, xx in ((w_high, xh), (w_high, xl), (w_low, xh)):
                        for h, (c0, cn) in enumerate(parts):
                            last_one = k == w_k + nk - 1 and w is w_low
                            base = 0 if xx is not o_high and xx is not o_low else -META
                            ins = nc.tensor.matmul(banks[:, bank + h, 0:cn], w[:, j, k, :],
                                                   xx[:, first_k + k, c0 + base:c0 + base + cn],
                                                   start=start and k == 0 and w is w_high and xx is xh,
                                                   stop=stop and last_one)
                if used:
                    ins.then_inc(w_used, 1)

            pe.wait_ge(consts_made, 1)
            pe.wait_ge(rows_ready, 1)
            for i, k in enumerate(("lam_re", "lam_im", "decay_arg", "angle")):
                ins = nc.tensor.transpose(banks[:, 5, i * PAIRS:(i + 1) * PAIRS], row[k][:], ident[0:PAIRS, 0:PAIRS])
            ins.then_inc(rows_t, 1)
            for s in range(T):
                pe.wait_ge(x_loaded[s // 2], 32)
                if s >= 2:
                    pe.wait_ge(res_copied, s - 1)
                for k in range(KB):
                    ins = nc.tensor.transpose(banks[:, 2 * (s % 2) + k // 4, (k % 4) * C:(k % 4 + 1) * C],
                                              xt[:, s, k * P:(k + 1) * P], ident[0:C, 0:C])
                ins.then_inc(res_t, 1)
            pe.wait_ge(bc_loaded, 96)
            for i, k in enumerate(("b_re", "b_im", "c_re", "c_im")):
                if i >= 2:
                    pe.wait_ge(nat_copied, i - 1)
                for q in range(GROUP):
                    if k[0] == "b":
                        src = braw[k][:].rearrange("r (n q) -> r n q", q=GROUP)[:, :, q]
                    else:
                        src = braw[k][:, q * P:(q + 1) * P]
                    ins = nc.tensor.transpose(banks[:, 4 + i % 2, q * PAIRS:(q + 1) * PAIRS], src, ident[0:PAIRS, 0:PAIRS])
                ins.then_inc(nat_tr, 1)
            pe.wait_ge(nat_copied, 3)
            pe.wait_ge(consts_loaded, 11 * 16)
            nc.tensor.transpose(banks[:, 4, 0:VECS], vecs_row[:], ident[0:VECS, 0:VECS]).then_inc(vecs_t, 1)
            for i in range(8):
                pe.wait_ge(u_normed, i // 2 + 1)
                if i < 2:
                    pe.wait_ge(res_copied, T)
                else:
                    pe.wait_ge(u_copied, i - 1)
                for g in range(8):
                    ins = nc.tensor.transpose(banks[:, 2 * (i % 2) + g // 4, (g % 4) * C:(g % 4 + 1) * C],
                                              u_row[:, i // 2 % 2, 8 * (i % 2) + g].rearrange("c s q -> c (s q)"),
                                              ident[0:C, 0:C])
                ins.then_inc(u_tr, 1)

            def injection(b):
                pe.wait_ge(inj_ready, b + 1)
                if b == 0:
                    pe.wait_ge(u_copied, 8)
                if b >= 1:
                    pe.wait_ge(inj_copied, b)
                for r_ in range(PB):
                    for i in range(2):
                        n = 2 * r_ + i
                        ins = nc.tensor.transpose(banks[:, n // 4, (n % 4) * P:(n % 4 + 1) * P],
                                                  inj[:, i, r_].rearrange("p s q -> p (s q)"), ident[:])
                ins.then_inc(inj_tr, 1)

            def additions(b):
                pe.wait_ge(inj_copied, b + 1)
                if b >= 1:
                    pe.wait_ge(v_taken, b)
                for r_ in range(PB):
                    for j in range(2):
                        for i in range(2):
                            ins = nc.tensor.matmul(banks[j * STATE:(j + 1) * STATE, 2 + i, r_ * CS:(r_ + 1) * CS],
                                                   inj_T[:, r_, i, j * STATE:(j + 1) * STATE],
                                                   u_state[:, b * GB + 2 * r_ + j, 0:CS], start=True, stop=True)
                ins.then_inc(v_ready, 1)

            def lags(b):
                pe.wait_ge(read_ready, b + 1)
                if b == 0:
                    pe.wait_ge(bbar_placed, 1)
                    pe.wait_ge(vecs_ready, 1)
                if b >= 2:
                    pe.wait_ge(k_copied, b - 1)
                for r_ in range(PB):
                    for i in range(2):
                        ins = nc.tensor.matmul(banks[0:2 * GROUP, 4 + b % 2, r_ * P:(r_ + 1) * P], bbar_pair[:, i, b * PB + r_, :],
                                               read[:, b % 3, i, r_, 0:T].rearrange("p t q -> p (t q)"),
                                               start=i == 0, stop=i == 1)
                ins.then_inc(k_ready, 1)

            def outputs(b):
                pe.wait_ge(toep_placed, 16 * T * (b + 1))
                pe.wait_ge(state_ready, b + 1)
                if b >= 1:
                    pe.wait_ge(gelu_ready, b)
                for g in range(GB):
                    r_, j = g // 2, g % 2
                    bank, c0 = 6 + j, r_ * C
                    nc.tensor.matmul(banks[:, bank, c0:c0 + C], k_toep[:, b % 2, j * PB + r_, :], u_state[:, b * GB + g, :],
                                     start=True, stop=False)
                    for i in range(2):
                        hs = slice(j * STATE, (j + 1) * STATE)
                        ins = nc.tensor.matmul(banks[:, bank, c0 + 1:c0 + C],
                                               read[hs, b % 3, i, r_, 1:T + 1].rearrange("p t q -> p (t q)"),
                                               state[hs, i, r_, :], start=False, stop=i == 1)
                ins.then_inc(y_ready, 1)

            def early_glu(off):
                product(QUAD_GLU, off, 0, GLU_EARLY, glu_high, glu_low, 2 * off, L, stop=False, used=False,
                        each=lambda k: pe.wait_ge(gt_split, k + 1))

            injection(0)
            lags(0)
            additions(0)
            for b in range(BATCHES):
                if b + 1 < BATCHES:
                    injection(b + 1)
                    lags(b + 1)
                    additions(b + 1)
                else:
                    early_glu(0)
                outputs(b)
            pe.wait_ge(v_taken, BATCHES)
            early_glu(1)
            for k in range(GLU_EARLY, KB):
                pe.wait_ge(gt_split, k + 1)
                for off in range(2):
                    product(QUAD_GLU, off, 0, 1, glu_high, glu_low, 2 * off, L, start=False, stop=k == KB - 1,
                            w_k=k, used=k == KB - 1)
            for i in range(N_GLU):
                for off in range(4):
                    if i > 0:
                        pe.wait_ge(gate_ready if off < 2 else up_taken, 2 * i + (off % 2 - 1))
                    elif off < 2:
                        continue
                    elif off == 3:
                        pe.wait_ge(gelu_ready, BATCHES)
                    product(QUAD_GLU + i, off, 0, KB, glu_high, glu_low, 2 * off, L)

            def mean(index, n):
                tt, nt, c0 = norm_tiles(n)
                pe.wait_ge(sq_added, KB * (index + 1))
                for t in range(nt):
                    ins = nc.tensor.matmul(banks[0:tt, 3 if index == 3 else 7, t:t + 1], sq_sum[:, c0 + t * tt:c0 + (t + 1) * tt], ones[:, 0:1],
                                           start=True, stop=True)
                ins.then_inc(mean_summed, 1)

            def spread(index, n):
                tt, nt, _ = norm_tiles(n)
                pe.wait_ge(diag_ready, index + 1)
                for t in range(nt):
                    o = rstd_banks(n)[:, t // 3, (t % 3) * tt:(t % 3 + 1) * tt] if n == L else rstd_banks(n)[:, t * tt:(t + 1) * tt]
                    ins = nc.tensor.matmul(o, ones[0:tt, :], diag[0:tt, t * tt:(t + 1) * tt], start=True, stop=True)
                ins.then_inc(rstd_spread, 1)

            def first_quad(quad, index, n, bank_free, up_free):
                for off in range(4):
                    if off < 2:
                        pe.wait_ge(*bank_free[off])
                    if off == 3:
                        pe.wait_ge(rstd_copied, index + 1)
                    if off >= 2 and up_free is not None:
                        pe.wait_ge(up_taken, up_free + off - 2)
                    product(quad, off, 0, KB, x_high, x_low, 2 * off, n,
                            each=(lambda k: pe.wait_ge(x_split, KB * index + k + 1)) if off == 0 else None)
                    if off == 0:
                        mean(index, n)
                    if off == 1:
                        spread(index, n)

            def feed_forward(layer, n, it0, adds0, index, bank_free):
                first_quad(QUAD_UP[layer], index, n, bank_free, 2 * it0 - 1 if layer == 0 else None)
                with pe.Fori(1, N_UP, 1) as i:
                    for off in range(4):
                        if off < 2:
                            pe.wait_ge(pre_ready, 2 * i + (2 * N_UP * layer + off - 1))
                        else:
                            pe.wait_ge(up_taken, 2 * i + (2 * it0 + off % 2 - 1))
                        product(QUAD_UP[layer] + i, off, 0, KB, x_high, x_low, 2 * off, n)

                def down(i):
                    q = QUAD_DOWN[layer] + 2 * i
                    for off in range(8):
                        k0, nk = DOWN_TILES[off // 2]
                        if off < 2:
                            pe.wait_ge(added, 2 * i + (adds0 - 1 + off))
                        if off == 2:
                            pe.wait_ge(a_split, 2 * N_UP * (layer + 1))
                        product(q, off, k0, nk, a_high, a_low, 2 * (off % 2), n, start=off < 2, stop=off >= 6)

                pe.wait_ge(pre_ready, 2 * N_UP * (layer + 1))
                pe.wait_ge(a_split, 2 * N_UP * (layer + 1) - 2)
                with pe.Fori(0, N_DOWN, 1) as i:
                    down(i)

            feed_forward(0, L, N_GLU, KB, 0, [(gate_ready, 2 * N_GLU - 1), (gate_ready, 2 * N_GLU)])
            first_quad(QUAD_KV, 1, L, [(added, 2 * KB - 1), (added, 2 * KB)], None)

            def query_block(i, half=None):
                if half != 1:
                    if i < 2:
                        pe.wait_ge(kv_scaled, 1)
                    else:
                        pe.wait_ge(q_scaled, i - 1)
                n = KB if half is None else KB // 2
                product(QUAD_Q, i, 0, n, x_high, x_low, i % 2, SEQ, start=half != 1, stop=half != 0,
                        w_k=KB // 2 if half == 1 else 0, used=half != 0)

            def scores(s):
                kv, b = s // BLOCKS, s % BLOCKS
                if b == 0:
                    pe.wait_ge(q_ready, 2 * kv + 2)
                if s >= 2:
                    pe.wait_ge(prob_t_ready, s - 1)
                for h, c in HALVES:
                    hs = slice(h * HD, (h + 1) * HD)
                    keys = k_t[hs, kv // 2, 0 if kv % 2 == h else 1, :]
                    chunk = 2 * b + c
                    for j in range(2):
                        q = q_t[hs, kv % 2, j, chunk * CHUNK:(chunk + 1) * CHUNK]
                        o = scores_of(s)[j * CHUNK:(j + 1) * CHUNK, h, c]
                        if chunk < 2:
                            ins = nc.tensor.matmul(o[:, 0:META + (chunk + 1) * CHUNK], q, keys[:, 0:META + (chunk + 1) * CHUNK], start=True, stop=True)
                        else:
                            first = META + (chunk - 1) * CHUNK
                            nc.tensor.matmul(o[:, 0:META], q, keys[:, 0:META], start=True, stop=True)
                            ins = nc.tensor.matmul(o[:, META:], q, keys[:, first:first + BAND], start=True, stop=True)
                ins.then_inc(scores_ready, 1)

            def transpose_probs(s):
                pe.wait_ge(prob_scaled, s + 1)
                if s >= 1:
                    pe.wait_ge(prob_t_ready, s)
                for i, (h, c) in enumerate(HALVES):
                    w = CHUNK if s % BLOCKS == 0 and c == 0 else BAND
                    nc.tensor.transpose(banks[0:w, 6, i * P:(i + 1) * P], prob_b[:, s % 2, i, 0:w], ident[:])
                nc.tensor.transpose(meta_of(s), prob_m[:, s % 2].rearrange("p i k -> p (i k)"),
                                    ident[:]).then_inc(prob_tr, 1)

            def values(s):
                kv, b = s // BLOCKS, s % BLOCKS
                vs = slice(kv * HD, (kv + 1) * HD)
                pe.wait_ge(prob_t_ready, s + 1)
                if s >= 1:
                    pe.wait_ge(o_split, s)
                for i, (h, c) in enumerate(HALVES):
                    chunk = 2 * b + c
                    w = CHUNK if chunk == 0 else BAND
                    o = banks[h * HD:(h + 1) * HD, 7, c * P:(c + 1) * P]
                    nc.tensor.matmul(o, v_win[0:w, max(chunk - 1, 0), vs], prob_tb[0:w, s % 2, i, :], start=True, stop=False)
                    ins = nc.tensor.matmul(o, v_meta[:, i, vs], prob_tm[:, s % 2, :], start=False, stop=True)
                ins.then_inc(o_ready, 1)

            query_block(0)
            query_block(1)
            pe.wait_ge(kv_ready, 4)
            for w in range(WINDOWS):
                for t in range(2):
                    nc.tensor.transpose(banks[:, 4 + w // 2, (w % 2) * 2 * P + t * P:(w % 2) * 2 * P + (t + 1) * P],
                                        v_t[:, t, META + w * CHUNK:META + w * CHUNK + BAND], ident[:])
            pe.wait_ge(v_meta_ready, 1)
            for i in range(4):
                for t in range(2):
                    ins = nc.tensor.transpose(banks[0:4 * META, 2 + i // 2, (i % 2) * 2 * P + t * P:(i % 2) * 2 * P + (t + 1) * P],
                                              v_meta_t[:, t, i, :], ident[:])
            ins.then_inc(v_tr, 1)
            query_block(2)
            pe.wait_ge(keys_swapped, 32)
            pe.wait_ge(v_rows_ready, 1)
            for s in range(STEPS + 2):
                if s < STEPS:
                    scores(s)
                if 1 <= s < STEPS + 1:
                    transpose_probs(s - 1)
                if s >= 2:
                    values(s - 2)
                if s < QUERY_STEPS:
                    query_block(FIRST_QUERIES + s // 2, s % 2)
                if s in WO_STEPS:
                    m, k0 = WO_STEPS[s]
                    if k0 == 0:
                        pe.wait_ge(q_scaled, KB - 1 + m)
                    pe.wait_ge(o_split, (k0 // 2 + 1) * BLOCKS)
                    product(QUAD_WO, m, 0, 2, o_high, o_low, m, SEQ, start=k0 == 0, stop=False, w_k=k0, used=False)
            pe.wait_ge(o_split, STEPS)
            for m in range(KB):
                if m >= 4:
                    pe.wait_ge(added, 2 * KB + m - 3)
                if m < 2:
                    product(QUAD_WO, m, 0, KB - WO_EARLY, o_high, o_low, m, SEQ, start=False, w_k=WO_EARLY)
                else:
                    product(QUAD_WO, m, 0, KB, o_high, o_low, m % 4, SEQ)
            feed_forward(1, SEQ, N_GLU + N_UP, 3 * KB, 2, [(added, 2 * KB + 5), (added, 2 * KB + 7)])
            for h in range(2):
                pe.wait_ge(scaled_ready, 4 * (h + 1))
                if h == 1:
                    mean(3, SEQ)
                for j in range(4):
                    if h == 1 and j == 3:
                        pe.wait_ge(mean_taken, 4)
                    for k in range(4):
                        ins = nc.tensor.transpose(banks[:, 4 * (1 - h) + j, k * P:(k + 1) * P],
                                                  scaled[:, 4 * h + k, META + j * P:META + (j + 1) * P], ident[:])
                    ins.then_inc(out_tr, 1)


_INS = ["x", "meta_tokens", "ln_mix", "ln_ffn", "ssm_lam_re", "ssm_lam_im", "ssm_log_dt", "ssm_b_re", "ssm_b_im",
        "ssm_c_re", "ssm_c_im", "ssm_d", "ssm_w_glu_a", "ssm_w_glu_b", "attn_w_qkv", "attn_b_qkv", "attn_sinks",
        "attn_w_o", "attn_b_o", "ffn_w_gate", "ffn_w_up", "ffn_w_down", "ln_f"]


def kernel(**inputs):
    import numpy as _np
    import concourse.bacc as _bacc
    from concourse import mybir as _mybir
    from concourse.bass_utils import run_bass_kernel_spmd as _run

    nc = _bacc.Bacc("TRN2", target_bir_lowering=False, num_devices=1)
    arrays, args = {}, []
    for name in _INS:
        a = _np.ascontiguousarray(inputs[name])
        arrays[f"in_{name}"] = a
        args.append(nc.dram_tensor(f"in_{name}", a.shape, _mybir.dt.from_np(a.dtype), kind="ExternalInput").ap())
    args.append(nc.dram_tensor("out", (1, SEQ, D), F32, kind="ExternalOutput").ap())
    trunk(nc, *args)
    r = _run(nc, [arrays], core_ids=[0])
    return r.results[0]["out"]
```
